# Optimizing a Trainium2 kernel written in Bass

```python
import math
import jax
import jax.numpy as jnp
from jax import lax
import numpy as np
import jax, jax.numpy as jnp

D_MODEL = 1024
BATCH = 1
SEQ = 256
DEPTH = 1

DA_HEADS = 8
DA_HEAD_DIM = 64
DA_V_DIM = 2 * DA_HEAD_DIM
DA_QK_WIDTH = DA_HEADS * 2 * DA_HEAD_DIM
DA_V_WIDTH = DA_HEADS * DA_V_DIM
DA_Q_BLOCK = 128
SSD_D_INNER = 2 * D_MODEL
SSD_HEAD_DIM = 64
SSD_HEADS = SSD_D_INNER // SSD_HEAD_DIM
SSD_GROUPS = 4
SSD_HEADS_PER_GROUP = SSD_HEADS // SSD_GROUPS
SSD_D_STATE = 128
SSD_BC_WIDTH = SSD_GROUPS * SSD_D_STATE
SSD_XBC_WIDTH = SSD_D_INNER + 2 * SSD_BC_WIDTH
SSD_CONV = 4
SSD_CHUNK = 256
DT_MIN = 0.001
DT_MAX = 0.1
N_BRANCHES = 2
IN_SPLITS = (DA_QK_WIDTH, DA_QK_WIDTH, DA_V_WIDTH, SSD_D_INNER, SSD_XBC_WIDTH, SSD_HEADS, N_BRANCHES * D_MODEL)
IN_WIDTH = sum(IN_SPLITS)
PEER_N_KEYS = 128
PEER_N_EXPERTS = PEER_N_KEYS * PEER_N_KEYS
PEER_HEADS = 8
PEER_TOPK = 16
PEER_QUERY_DIM = 256
PEER_HALF_DIM = PEER_QUERY_DIM // 2
PEER_TOKEN_BLOCK = 512
ALPHA = (2 * DEPTH) ** 0.25
BETA = (8 * DEPTH) ** -0.25
EPS = 1e-5


def layer_norm(x, g, b):
    xf = x.astype(jnp.float32)
    mu = jnp.mean(xf, axis=-1, keepdims=True)
    var = jnp.mean(jnp.square(xf - mu), axis=-1, keepdims=True)
    return ((xf - mu) * lax.rsqrt(var + EPS) * g + b).astype(x.dtype)

def rms_norm(x, w):
    xf = x.astype(jnp.float32)
    return (xf * lax.rsqrt(jnp.mean(jnp.square(xf), axis=-1, keepdims=True) + EPS) * w).astype(x.dtype)

def alibi_slopes(n):
    return jnp.asarray([2.0 ** (-8.0 * (i + 1) / n) for i in range(n)], jnp.float32)

def diff_attention(q, k, v, lam, lambda_init, subln_w):
    bsz, s = q.shape[:2]
    scale = DA_HEAD_DIM ** -0.5
    slopes = alibi_slopes(DA_HEADS)
    outs = []
    for i in range(s // DA_Q_BLOCK):
        q0 = i * DA_Q_BLOCK
        kend = q0 + DA_Q_BLOCK
        scores = jnp.einsum('bqhjd,bkhjd->bhjqk', q[:, q0:kend], k[:, :kend]).astype(jnp.float32) * scale
        dist = (jnp.arange(q0, kend)[:, None] - jnp.arange(kend)[None, :]).astype(jnp.float32)
        bias = jnp.where(dist[None] >= 0, -slopes[:, None, None] * dist[None], -jnp.inf)
        p = jax.nn.softmax(scores + bias[None, :, None], axis=-1)
        a = p[:, :, 0] - lam * p[:, :, 1]
        outs.append(jnp.einsum('bhqk,bkhe->bqhe', a.astype(v.dtype), v[:, :kend]))
    o = jnp.concatenate(outs, axis=1)
    o = rms_norm(o, subln_w) * (1.0 - lambda_init)
    return o.reshape(bsz, s, DA_V_WIDTH)

def causal_depthwise_conv(u, w, b):
    out = lax.conv_general_dilated(u, w[:, None, :].astype(u.dtype), window_strides=(1,),
                                   padding=[(SSD_CONV - 1, 0)], dimension_numbers=('NWC', 'WIO', 'NWC'),
                                   feature_group_count=u.shape[-1])
    return out + b

def ssd_chunked_scan(xh, dt, a, b_in, c_in):
    bsz, s = xh.shape[:2]
    pad = (-s) % SSD_CHUNK
    def padt(t):
        return jnp.pad(t, [(0, 0), (0, pad)] + [(0, 0)] * (t.ndim - 2))
    xh, dt, b_in, c_in = padt(xh), padt(dt), padt(b_in), padt(c_in)
    n_chunks = (s + pad) // SSD_CHUNK
    r = SSD_HEADS_PER_GROUP
    def chunks(t, tail):
        return t.reshape((bsz, n_chunks, SSD_CHUNK) + tail).swapaxes(0, 1)
    xs = (chunks(xh, (SSD_GROUPS, r, SSD_HEAD_DIM)), chunks(dt, (SSD_GROUPS, r)),
          chunks(b_in, (SSD_GROUPS, SSD_D_STATE)), chunks(c_in, (SSD_GROUPS, SSD_D_STATE)))
    a_gr = a.reshape(SSD_GROUPS, r)
    causal = jnp.tril(jnp.ones((SSD_CHUNK, SSD_CHUNK), dtype=bool))[None, :, :, None, None]

    def step(state, inp):
        xc, dtc, bc, cc = inp
        cum = jnp.cumsum(dtc * a_gr, axis=1)
        seg = cum[:, :, None] - cum[:, None, :]
        decay_ts = jnp.exp(jnp.where(causal, seg, -jnp.inf))
        cb = jnp.einsum('btgn,bsgn->btsg', cc, bc)
        w = cb[..., None] * decay_ts * dtc[:, None]
        y = jnp.einsum('btsgr,bsgrp->btgrp', w, xc)
        y = y + jnp.einsum('btgn,bgrpn->btgrp', cc, state) * jnp.exp(cum)[..., None]
        decay_end = jnp.exp(cum[:, -1:] - cum) * dtc
        state = state * jnp.exp(cum[:, -1])[..., None, None] + jnp.einsum('bsgn,bsgrp->bgrpn', bc, decay_end[..., None] * xc)
        return state, y

    state0 = jnp.zeros((bsz, SSD_GROUPS, r, SSD_HEAD_DIM, SSD_D_STATE), jnp.float32)
    _, ys = lax.scan(step, state0, xs)
    ys = ys.swapaxes(0, 1).reshape(bsz, n_chunks * SSD_CHUNK, SSD_HEADS, SSD_HEAD_DIM)
    return ys[:, :s]

def mamba2_branch(z, xbc, dt_raw, conv_w, conv_b, dt_bias, a_log, d_skip, norm_w):
    bsz, s = z.shape[:2]
    f32 = jnp.float32
    xbc = jax.nn.silu(causal_depthwise_conv(xbc, conv_w, conv_b))
    xs, b_in, c_in = jnp.split(xbc, [SSD_D_INNER, SSD_D_INNER + SSD_BC_WIDTH], axis=-1)
    xh = xs.reshape(bsz, s, SSD_HEADS, SSD_HEAD_DIM).astype(f32)
    dt = jax.nn.softplus(dt_raw.astype(f32) + dt_bias)
    a = -jnp.exp(a_log.astype(f32))
    y = ssd_chunked_scan(xh, dt, a,
                         b_in.reshape(bsz, s, SSD_GROUPS, SSD_D_STATE).astype(f32),
                         c_in.reshape(bsz, s, SSD_GROUPS, SSD_D_STATE).astype(f32))
    y = y + d_skip.astype(f32)[:, None] * xh
    y = y.reshape(bsz, s, SSD_D_INNER) * jax.nn.silu(z.astype(f32))
    y = rms_norm(y.reshape(bsz, s, SSD_GROUPS, SSD_D_INNER // SSD_GROUPS),
                 norm_w.reshape(SSD_GROUPS, -1)).reshape(bsz, s, SSD_D_INNER)
    return y.astype(z.dtype)

def peer_ffn(h, w_query, sub_keys, expert_u, expert_v):
    bsz, s, d = h.shape
    n_tok = bsz * s
    pad = (-n_tok) % PEER_TOKEN_BLOCK
    blocks = jnp.pad(h.reshape(n_tok, d), ((0, pad), (0, 0))).reshape(-1, PEER_TOKEN_BLOCK, d)

    def one_block(tb):
        q = (tb @ w_query).reshape(-1, PEER_HEADS, 2, PEER_HALF_DIM)
        sc = jnp.einsum('thjd,jkd->thjk', q, sub_keys).astype(jnp.float32)
        val, idx = lax.top_k(sc, PEER_TOPK)
        cand_s = val[:, :, 0, :, None] + val[:, :, 1, None, :]
        cand_i = idx[:, :, 0, :, None] * PEER_N_KEYS + idx[:, :, 1, None, :]
        cand_s = cand_s.reshape(cand_s.shape[0], PEER_HEADS, PEER_TOPK * PEER_TOPK)
        cand_i = cand_i.reshape(cand_i.shape[0], PEER_HEADS, PEER_TOPK * PEER_TOPK)
        top_s, pos = lax.top_k(cand_s, PEER_TOPK)
        eidx = jnp.take_along_axis(cand_i, pos, axis=-1)
        g = jax.nn.softmax(top_s, axis=-1)
        act = jax.nn.gelu(jnp.einsum('thkd,td->thk', expert_u[eidx], tb), approximate=False)
        wts = (g * act.astype(jnp.float32)).astype(tb.dtype)
        return jnp.einsum('thk,thkd->td', wts, expert_v[eidx])

    out = lax.map(one_block, blocks)
    return out.reshape(-1, d)[:n_tok].reshape(bsz, s, d)

def first_inputs(seed: int = 0) -> dict:
    key = jax.random.key(seed)
    ks = jax.random.split(key, 28)
    f32 = jnp.float32
    L = DEPTH
    def nrm(k, shape, std):
        return jax.random.normal(k, shape, f32) * std
    dt0 = jnp.exp(jax.random.uniform(ks[7], (L, SSD_HEADS), f32) * (math.log(DT_MAX) - math.log(DT_MIN)) + math.log(DT_MIN))
    return {
        'x': nrm(ks[0], (BATCH, SEQ, D_MODEL), 1.0),
        'c': nrm(ks[1], (BATCH, D_MODEL), 1.0),
        'w_ada': nrm(ks[2], (L, D_MODEL, 6 * D_MODEL), 0.5 * D_MODEL ** -0.5),
        'b_ada': nrm(ks[3], (L, 6 * D_MODEL), 0.02),
        'w_in': nrm(ks[4], (L, D_MODEL, IN_WIDTH), D_MODEL ** -0.5),
        'conv_w': nrm(ks[5], (L, SSD_CONV, SSD_XBC_WIDTH), SSD_CONV ** -0.5),
        'conv_b': nrm(ks[6], (L, SSD_XBC_WIDTH), 0.02),
        'dt_bias': dt0 + jnp.log(-jnp.expm1(-dt0)),
        'a_log': jnp.log(jax.random.uniform(ks[8], (L, SSD_HEADS), f32, 1.0, 16.0)),
        'd_skip': 1.0 + nrm(ks[9], (L, SSD_HEADS), 0.1),
        'ssd_norm_w': 1.0 + nrm(ks[10], (L, SSD_D_INNER), 0.1),
        'lambda_q1': nrm(ks[11], (L, DA_HEAD_DIM), 0.1),
        'lambda_k1': nrm(ks[12], (L, DA_HEAD_DIM), 0.1),
        'lambda_q2': nrm(ks[13], (L, DA_HEAD_DIM), 0.1),
        'lambda_k2': nrm(ks[14], (L, DA_HEAD_DIM), 0.1),
        'da_subln_w': 1.0 + nrm(ks[15], (L, DA_V_DIM), 0.1),
        'w_attn_branch': nrm(ks[16], (L, DA_V_WIDTH, D_MODEL), DA_V_WIDTH ** -0.5),
        'w_ssd_branch': nrm(ks[17], (L, SSD_D_INNER, D_MODEL), SSD_D_INNER ** -0.5),
        'w_out': nrm(ks[18], (L, D_MODEL, D_MODEL), BETA * D_MODEL ** -0.5),
        'ln1_g': 1.0 + nrm(ks[19], (L, D_MODEL), 0.1),
        'ln1_b': nrm(ks[20], (L, D_MODEL), 0.02),
        'peer_w_query': nrm(ks[21], (L, D_MODEL, PEER_HEADS * PEER_QUERY_DIM), D_MODEL ** -0.5),
        'peer_sub_keys': nrm(ks[22], (L, 2, PEER_N_KEYS, PEER_HALF_DIM), PEER_HALF_DIM ** -0.5),
        'peer_u': nrm(ks[23], (L, PEER_N_EXPERTS, D_MODEL), D_MODEL ** -0.5),
        'peer_v': nrm(ks[24], (L, PEER_N_EXPERTS, D_MODEL), BETA * PEER_HEADS ** -0.5),
        'ln2_g': 1.0 + nrm(ks[25], (L, D_MODEL), 0.1),
        'ln2_b': nrm(ks[26], (L, D_MODEL), 0.02),
    }

def first_block(x, c, w_ada, b_ada, w_in, conv_w, conv_b, dt_bias, a_log, d_skip, ssd_norm_w,
              lambda_q1, lambda_k1, lambda_q2, lambda_k2, da_subln_w, w_attn_branch, w_ssd_branch,
              w_out, ln1_g, ln1_b, peer_w_query, peer_sub_keys, peer_u, peer_v, ln2_g, ln2_b):
    bsz, s, _ = x.shape
    split_at = np.cumsum(IN_SPLITS)[:-1].tolist()
    f32 = jnp.float32
    for l in range(DEPTH):
        mod = jax.nn.silu(c) @ w_ada[l] + b_ada[l]
        shift1, scale1, gate1, shift2, scale2, gate2 = jnp.split(mod[:, None, :], 6, axis=-1)
        h = x * (1.0 + scale1) + shift1
        q, k, v, z, xbc, dt_raw, g_logits = jnp.split(h @ w_in[l], split_at, axis=-1)
        lambda_init = 0.8 - 0.6 * math.exp(-0.3 * l)
        lam = (jnp.exp(jnp.sum(lambda_q1[l].astype(f32) * lambda_k1[l].astype(f32)))
               - jnp.exp(jnp.sum(lambda_q2[l].astype(f32) * lambda_k2[l].astype(f32))) + lambda_init)
        y_attn = diff_attention(q.reshape(bsz, s, DA_HEADS, 2, DA_HEAD_DIM),
                                k.reshape(bsz, s, DA_HEADS, 2, DA_HEAD_DIM),
                                v.reshape(bsz, s, DA_HEADS, DA_V_DIM),
                                lam, lambda_init, da_subln_w[l]) @ w_attn_branch[l]
        y_ssd = mamba2_branch(z, xbc, dt_raw, conv_w[l], conv_b[l], dt_bias[l], a_log[l],
                              d_skip[l], ssd_norm_w[l]) @ w_ssd_branch[l]
        g_attn, g_ssd = jnp.split(jax.nn.sigmoid(g_logits), N_BRANCHES, axis=-1)
        mixed = (g_attn * y_attn + g_ssd * y_ssd) @ w_out[l]
        x = layer_norm(ALPHA * x + gate1 * mixed, ln1_g[l], ln1_b[l])
        h2 = x * (1.0 + scale2) + shift2
        y_ffn = peer_ffn(h2, peer_w_query[l], peer_sub_keys[l], peer_u[l], peer_v[l])
        x = layer_norm(ALPHA * x + gate2 * y_ffn, ln2_g[l], ln2_b[l])
    return x


DEPTH_2 = 2

N_MIXERS = 2
N_REC_LAYERS = (DEPTH_2 + 1) // 2
N_ATT_LAYERS = DEPTH_2 // 2
EPS_2 = 1e-6

D_RNN = D_MODEL
RG_BLOCKS = 4
RG_BW = D_RNN // RG_BLOCKS
CONV_W = 4
RG_C = 8.0

H_ATT = 16
D_QK = 64
D_V = 64
D_LAT = 128
H_IDX = 8
D_IDX = 64
TOPK_MAX = 256
Q_BLOCK = 128
ATT_SCALE = D_QK ** -0.5
IDX_W_SCALE = (H_IDX ** -0.5) * (D_IDX ** -0.5)
ATT_IN_SPLITS = [H_ATT * D_QK,
                 H_ATT * D_QK + D_LAT,
                 H_ATT * D_QK + D_LAT + H_IDX * D_IDX,
                 H_ATT * D_QK + D_LAT + H_IDX * D_IDX + D_IDX]
ATT_IN_DIM = ATT_IN_SPLITS[-1] + H_IDX

NUM_BUCKETS = 32
MAX_DISTANCE = 128
MAX_EXACT = NUM_BUCKETS // 2

D_FF = 4 * D_MODEL


def rms_norm_2(x, g):
    xf = x.astype(jnp.float32)
    y = xf * lax.rsqrt(jnp.mean(xf * xf, axis=-1, keepdims=True) + EPS_2)
    return (y * g.astype(jnp.float32)).astype(x.dtype)

def t5_bucket(dist):
    n = jnp.maximum(dist, 0)
    nf = jnp.maximum(n, 1).astype(jnp.float32)
    large = MAX_EXACT + (jnp.log(nf / MAX_EXACT) / math.log(MAX_DISTANCE / MAX_EXACT)
                         * (NUM_BUCKETS - MAX_EXACT)).astype(jnp.int32)
    large = jnp.minimum(large, NUM_BUCKETS - 1)
    return jnp.where(n < MAX_EXACT, n, large)

def rglru_mixer(h, w_in, conv_w, conv_b, w_a, b_a, w_x, b_x, lam, w_out):
    B, S, _ = h.shape
    gate, xr = jnp.split(h @ w_in, 2, axis=-1)
    gate = jax.nn.gelu(gate)
    xpad = jnp.pad(xr, ((0, 0), (CONV_W - 1, 0), (0, 0)))
    xc = conv_b + xpad[:, 0:S] * conv_w[0]
    for k in range(1, CONV_W):
        xc = xc + xpad[:, k:k + S] * conv_w[k]
    xb = xc.reshape(B, S, RG_BLOCKS, RG_BW)
    r = jax.nn.sigmoid(jnp.einsum('bsnj,nji->bsni', xb, w_a).reshape(B, S, D_RNN) + b_a)
    i = jax.nn.sigmoid(jnp.einsum('bsnj,nji->bsni', xb, w_x).reshape(B, S, D_RNN) + b_x)
    log_a = (-RG_C * r.astype(jnp.float32)) * jax.nn.softplus(-lam.astype(jnp.float32))
    a = jnp.exp(log_a)
    u = jnp.sqrt(-jnp.expm1(2.0 * log_a)) * (i * xc).astype(jnp.float32)

    def combine(left, right):
        a_l, b_l = left
        a_r, b_r = right
        return a_l * a_r, a_r * b_l + b_r

    _, hs = lax.associative_scan(combine, (a, u), axis=1)
    y = hs.astype(h.dtype) * gate
    return y @ w_out

def dsa_mixer(h, w_in, kv_norm_g, w_uk, w_uv, w_o, rel_bias):
    B, S, _ = h.shape
    n_blk = S // Q_BLOCK
    topk = min(TOPK_MAX, S // 4)
    q, c, qi, ki, wi = jnp.split(h @ w_in, ATT_IN_SPLITS, axis=-1)
    q = q.reshape(B, S, H_ATT, D_QK)
    c = rms_norm_2(c, kv_norm_g)
    qi = qi.reshape(B, S, H_IDX, D_IDX)
    wi = wi * IDX_W_SCALE
    q_lat = jnp.einsum('bshd,hdc->bshc', q, w_uk) * ATT_SCALE
    key_pos = jnp.arange(S)

    def block(args):
        q_lat_b, qi_b, wi_b, pos_b = args
        dots = jax.nn.relu(jnp.einsum('bqhd,bsd->bqhs', qi_b, ki))
        score = jnp.einsum('bqh,bqhs->bqs', wi_b, dots).astype(jnp.float32)
        causal = key_pos[None, :] <= pos_b[:, None]
        score = jnp.where(causal[None], score, -jnp.inf)
        _, idx = lax.top_k(score, topk)
        c_sel = jax.vmap(lambda cb, ib: cb[ib])(c, idx)
        dist = pos_b[None, :, None] - idx
        bias = jnp.moveaxis(rel_bias[t5_bucket(dist)], -1, 2)
        logits = jnp.einsum('bqhc,bqkc->bqhk', q_lat_b, c_sel).astype(jnp.float32) \
            + bias.astype(jnp.float32)
        logits = jnp.where((dist >= 0)[:, :, None, :], logits, -jnp.inf)
        p = jax.nn.softmax(logits, axis=-1).astype(c.dtype)
        return jnp.einsum('bqhk,bqkc->bqhc', p, c_sel)

    def to_blocks(a):
        return a.reshape(B, n_blk, Q_BLOCK, *a.shape[2:]).swapaxes(0, 1)

    o_lat = lax.map(block, (to_blocks(q_lat), to_blocks(qi), to_blocks(wi),
                            key_pos.reshape(n_blk, Q_BLOCK)))
    o_lat = o_lat.swapaxes(0, 1).reshape(B, S, H_ATT, D_LAT)
    o = jnp.einsum('bshc,hcv->bshv', o_lat, w_uv).reshape(B, S, H_ATT * D_V)
    return o @ w_o

def sq_relu_mlp(h, w_up, w_down):
    return jnp.square(jax.nn.relu(h @ w_up)) @ w_down

def second_inputs(seed: int = 0) -> dict:
    key = jax.random.key(seed)
    ks = jax.random.split(key, 24)
    nr, na, L = N_REC_LAYERS, N_ATT_LAYERS, DEPTH_2
    f32 = jnp.float32

    def nrm(k, shape, scale):
        return jax.random.normal(k, shape, f32) * scale

    u = jax.random.uniform(ks[10], (nr, D_RNN), f32, 0.9, 0.999)
    return {
        "x": jax.random.normal(ks[0], (BATCH, SEQ, D_MODEL), f32),
        "norm_mix_g": 1.0 + nrm(ks[1], (L, D_MODEL), 0.02),
        "norm_mlp_g": 1.0 + nrm(ks[2], (L, D_MODEL), 0.02),
        "final_norm_g": 1.0 + nrm(ks[3], (D_MODEL,), 0.02),
        "rec_w_in": nrm(ks[4], (nr, D_MODEL, 2 * D_RNN), D_MODEL ** -0.5),
        "rec_conv_w": nrm(ks[5], (nr, CONV_W, D_RNN), CONV_W ** -0.5),
        "rec_conv_b": nrm(ks[6], (nr, D_RNN), 0.01),
        "rec_w_a": nrm(ks[7], (nr, RG_BLOCKS, RG_BW, RG_BW), RG_BW ** -0.5),
        "rec_b_a": nrm(ks[8], (nr, D_RNN), 0.01),
        "rec_w_x": nrm(ks[9], (nr, RG_BLOCKS, RG_BW, RG_BW), RG_BW ** -0.5),
        "rec_b_x": nrm(ks[11], (nr, D_RNN), 0.01),
        "rec_lambda": jnp.log(u) - jnp.log1p(-u),
        "rec_w_out": nrm(ks[12], (nr, D_RNN, D_MODEL), D_RNN ** -0.5),
        "att_w_in": nrm(ks[13], (na, D_MODEL, ATT_IN_DIM), D_MODEL ** -0.5),
        "att_kv_norm_g": 1.0 + nrm(ks[14], (na, D_LAT), 0.02),
        "att_w_uk": nrm(ks[15], (na, H_ATT, D_QK, D_LAT), D_LAT ** -0.5),
        "att_w_uv": nrm(ks[16], (na, H_ATT, D_LAT, D_V), D_LAT ** -0.5),
        "att_w_o": nrm(ks[17], (na, H_ATT * D_V, D_MODEL), (H_ATT * D_V) ** -0.5),
        "rel_bias": nrm(ks[18], (NUM_BUCKETS, H_ATT), 0.2),
        "mlp_w_up": nrm(ks[19], (L, D_MODEL, D_FF), D_MODEL ** -0.5),
        "mlp_w_down": nrm(ks[20], (L, D_FF, D_MODEL), D_FF ** -0.5),
    }

def second_block(x, norm_mix_g, norm_mlp_g, final_norm_g,
              rec_w_in, rec_conv_w, rec_conv_b, rec_w_a, rec_b_a, rec_w_x, rec_b_x,
              rec_lambda, rec_w_out,
              att_w_in, att_kv_norm_g, att_w_uk, att_w_uv, att_w_o, rel_bias,
              mlp_w_up, mlp_w_down):
    for layer in range(DEPTH_2):
        j = layer // N_MIXERS
        hn = rms_norm_2(x, norm_mix_g[layer])
        if layer % N_MIXERS == 0:
            mix = rglru_mixer(hn, rec_w_in[j], rec_conv_w[j], rec_conv_b[j],
                              rec_w_a[j], rec_b_a[j], rec_w_x[j], rec_b_x[j],
                              rec_lambda[j], rec_w_out[j])
        else:
            mix = dsa_mixer(hn, att_w_in[j], att_kv_norm_g[j], att_w_uk[j],
                            att_w_uv[j], att_w_o[j], rel_bias)
        x = x + mix
        x = x + sq_relu_mlp(rms_norm_2(x, norm_mlp_g[layer]), mlp_w_up[layer], mlp_w_down[layer])
    return rms_norm_2(x, final_norm_g)


def setup_inputs(seed=0):
    out = dict(first_inputs(seed))
    for name, value in second_inputs(seed + 1).items():
        if name != "x":
            out[name + "_2"] = value
    return out


def reference(
    x, c, w_ada, b_ada, w_in, conv_w, conv_b, dt_bias, a_log, d_skip, ssd_norm_w, lambda_q1,
    lambda_k1, lambda_q2, lambda_k2, da_subln_w, w_attn_branch, w_ssd_branch, w_out, ln1_g,
    ln1_b, peer_w_query, peer_sub_keys, peer_u, peer_v, ln2_g, ln2_b, norm_mix_g_2,
    norm_mlp_g_2, final_norm_g_2, rec_w_in_2, rec_conv_w_2, rec_conv_b_2, rec_w_a_2, rec_b_a_2,
    rec_w_x_2, rec_b_x_2, rec_lambda_2, rec_w_out_2, att_w_in_2, att_kv_norm_g_2, att_w_uk_2,
    att_w_uv_2, att_w_o_2, rel_bias_2, mlp_w_up_2, mlp_w_down_2,
):
    x = first_block(
        x, c, w_ada, b_ada, w_in, conv_w, conv_b, dt_bias, a_log, d_skip, ssd_norm_w, lambda_q1,
        lambda_k1, lambda_q2, lambda_k2, da_subln_w, w_attn_branch, w_ssd_branch, w_out, ln1_g,
        ln1_b, peer_w_query, peer_sub_keys, peer_u, peer_v, ln2_g, ln2_b,
    )
    return second_block(
        x, norm_mix_g_2, norm_mlp_g_2, final_norm_g_2, rec_w_in_2, rec_conv_w_2, rec_conv_b_2,
        rec_w_a_2, rec_b_a_2, rec_w_x_2, rec_b_x_2, rec_lambda_2, rec_w_out_2, att_w_in_2,
        att_kv_norm_g_2, att_w_uk_2, att_w_uv_2, att_w_o_2, rel_bias_2, mlp_w_up_2,
        mlp_w_down_2,
    )


_drawn_inputs = setup_inputs


def setup_inputs(seed=0):
    import zlib

    import numpy as np

    out = dict(_drawn_inputs(seed))
    spreads = {}
    factors = {'b_ada': 3.083,
     'conv_b': 8.0,
     'd_skip': 5.095,
     'ssd_norm_w': 3.871,
     'lambda_q1': 3.062,
     'lambda_k1': 6.973,
     'lambda_q2': 6.687,
     'lambda_k2': 8.0,
     'da_subln_w': 3.752,
     'norm_mix_g_2': 2.744,
     'final_norm_g_2': 2.83,
     'rec_conv_b_2': 3.11,
     'rec_b_a_2': 8.0,
     'rec_b_x_2': 8.0,
     'att_kv_norm_g_2': 8.0}
    for name, (base, spread) in spreads.items():
        noise = np.random.default_rng([zlib.crc32(name.encode()), seed]).standard_normal(out[name].shape)
        drawn = base * np.exp(spread * noise) if base else spread * noise
        out[name] = jnp.asarray(drawn.astype(out[name].dtype))
    for name, factor in factors.items():
        out[name] = (out[name] * factor).astype(out[name].dtype)
    return out
```

```python
import math
from contextlib import ExitStack

import concourse.bass as bass
import numpy as np
from concourse import mybir

F32 = mybir.dt.float32
U32 = mybir.dt.uint32
ALU = mybir.AluOpType
ACT = mybir.ActivationFunctionType
AX = mybir.AxisListType

P = 128
TOK = 256
TT = TOK // P
D = 1024
DC = D // P
COLS = 256
SLOTS = 4
TILE = DC * COLS
NEG = -3.0e38
FAR = 1.0e30

HEADS = 8
DA_SCALE = 64 ** -0.5
LAMBDA_INIT = 0.8 - 0.6 * math.exp(0.0)
SSD_HEADS = 32
GROUPS = 4
EPS = 1e-5
EPS_2 = 1e-6
ALPHA = 2.0 ** 0.25
TOPK = 16
EXPERTS = 128 * 128
RG_C = 8.0
H_ATT = 16
H_IDX = 8
ATT_SCALE = 64 ** -0.5
IDX_W_SCALE = (8 ** -0.5) * (64 ** -0.5)
KEEP = 64
BUCKETS = 32
WIDE = P + TOK

STREAM = [("q", 1, 4), ("k", 1, 4), ("v", 1, 4), ("xbc", 1, 12), ("z", 1, 8), ("g", 1, 8),
          ("attn", 1, 4), ("ssd", 2, 4), ("out", 1, 4), ("query", 1, 8),
          ("rec_in", 1, 8), ("rec_out", 1, 4), ("up0", 1, 16), ("down0", 4, 4),
          ("att_in", 1, 7), ("uk_uv", 1, 1), ("att_out", 1, 4), ("up1", 1, 16), ("down1", 4, 4)]
TILE0, COLT0 = {}, {}


def _number_tiles():
    tile, colt = 0, 0
    for name, groups, cols in STREAM:
        TILE0[name], COLT0[name] = tile, colt
        tile += groups * cols
        colt += 0 if name == "uk_uv" else cols
    return tile


N_TILES = _number_tiles()

PARAMS = [("b_ada", 48), ("conv_w", 96), ("conv_b", 24), ("ssd_norm_w", 16), ("d_skip", 16), ("subln", 1),
          ("ln1_g", 8), ("ln1_b", 8), ("ln2_g", 8), ("ln2_b", 8), ("mix_g", 16), ("mlp_g", 16), ("final_g", 8),
          ("rec_conv_w", 32), ("rec_conv_b", 8), ("rec_b_a", 8), ("rec_b_x", 8), ("rec_lambda", 8),
          ("kv_g", 1), ("c", 8)]
ROWS = [("dt_bias", 32), ("a_log", 32), ("lambda_q1", 64), ("lambda_k1", 64), ("lambda_q2", 64), ("lambda_k2", 64)]
CONSTS = [("ident", P), ("ones", P), ("dist", WIDE), ("triu", TOK), ("iota", TOPK), ("flip", P)]


def offsets(table):
    at, out = 0, {}
    for name, n in table:
        out[name] = (at, at + n)
        at += n
    return out, at


def plan_jobs():
    jobs = ["mod_a"]
    jobs += [("s", 0, 0), ("s", 0, 1)]
    for h in range(HEADS):
        if h == 1:
            jobs.append("dt")
        if h == 4:
            jobs += ["mod_b", "cum0", "cum1"]
        jobs.append(("t", h))
        if h + 1 < HEADS:
            jobs += [("s", h + 1, 0), ("s", h + 1, 1)]
        jobs.append(("o", h))
    jobs += [("yn", h) for h in range(HEADS)]
    jobs += [("xs", i) for i in range(8)] + [("cb", g) for g in range(GROUPS)]
    jobs += [("cr", 0), ("cr", 1)]
    for pair in range(SSD_HEADS // 2):
        if pair + 1 < SSD_HEADS // 2:
            jobs += [("cr", 2 * pair + 2), ("cr", 2 * pair + 3)]
        jobs.append(("y", pair))
    jobs += [("gn", g) for g in range(GROUPS)]
    jobs += ["mean1", "var1"]
    jobs += [("h2", i) for i in range(4)]
    jobs += [("sc", c) for c in range(16)]
    jobs += [("yt", i) for i in range(4)] + ["mean2", "var2"]
    jobs += ["rms_mix0"] + [("rg", c) for c in range(8)] + ["rms_mlp0"]
    jobs += ["bv", "rms_mix1", "wi", "rms_c", "ctok"] + [("dot", h) for h in range(H_IDX)]
    jobs += [("ql", h) for h in range(H_ATT)]
    jobs += [("lg", 0), ("lg", 1)]
    for h in range(H_ATT):
        if h + 2 < H_ATT:
            jobs.append(("lg", h + 2))
        jobs += [("pt", h), ("ol", h)]
        if h % 2 == 1:
            jobs.append(("ot", h // 2))
    jobs += ["rms_mlp1", "rms_fin"]
    return {name: n for n, name in enumerate(jobs)}


JOBS = plan_jobs()


def program(nc, io):
    PO, NPAR = offsets(PARAMS)
    RO, NROW = offsets(ROWS)
    CO, NCON = offsets(CONSTS)
    ctx = ExitStack()
    with ctx:
        def sb(name, shape, dt=F32):
            return ctx.enter_context(nc.sbuf_tensor(name, shape, dt))

        sems = {}

        def S(name):
            if name not in sems:
                sems[name] = ctx.enter_context(nc.semaphore(name))
            return sems[name]

        ring = sb("ring", [P, SLOTS, TILE])
        X = sb("X", [P, DC, TOK])
        H = sb("H", [P, DC, TOK])
        PROJ = sb("PROJ", [P, 72, TOK])
        V = sb("V", [P, TT, D])
        CONV = sb("CONV", [P, 24, TOK])
        AUX = sb("AUX", [P, 32, TOK])
        SCR = sb("SCR", [P, 3840])
        par = sb("par", [P, NPAR])
        con = sb("con", [P, NCON])
        mod = sb("mod", [P, 48])
        dts = sb("dts", [P, 7, TT, 32])
        small = sb("small", [P, 256])
        wdt = PROJ[:, 71, :].rearrange("p (k n) -> p k n", k=DC)
        rows = PROJ[:, 69:71, :].rearrange("p a b -> p (a b)")[:, 0:NROW]
        RS = AUX[:, 31, :]
        PS = ctx.enter_context(nc.psum_tensor("PS", [P, 8, 512], F32))

        def pc(name, i=0, n=1):
            a = PO[name][0] + i
            return par[:, a:a + n]

        def row(name):
            return rows[:, RO[name][0]:RO[name][1]]

        def cst(name, a=0, b=None):
            return con[:, CO[name][0] + a:CO[name][1] if b is None else CO[name][0] + b]

        ident, ones = cst("ident"), cst("ones")

        def flat(ap):
            return ap.rearrange("p a b -> p (a b)")

        def over(ap, n):
            return ap.rearrange("p (o k) -> p o k", o=1).broadcast_to([P, n, ap.shape[1]])

        def each(ap, n):
            return ap.rearrange("p a (b o) -> p a b o", o=1).broadcast_to([P, ap.shape[1], ap.shape[2], n])

        Q, K, Z, XBC, G = (PROJ[:, a:b, :] for a, b in ((0, 8), (8, 16), (16, 32), (32, 56), (56, 72)))
        YA, MIX, YS = PROJ[:, 0:8, :], PROJ[:, 8:16, :], PROJ[:, 32:48, :]
        SC = [[SCR[:, (2 * b + j) * WIDE:(2 * b + j + 1) * WIDE] for j in range(2)] for b in range(2)]
        AM = [SCR[:, (4 + b) * WIDE:(5 + b) * WIDE] for b in range(2)]
        AT = [SCR[:, (6 + b) * WIDE:(7 + b) * WIDE] for b in range(2)]
        AB = [SCR[:, (8 + b) * WIDE:(9 + b) * WIDE] for b in range(2)]
        adaW = AUX[:, :, :].rearrange("p (s k) n -> p s k n", s=SLOTS)
        XDT = flat(AUX[:, 0:16, :]).rearrange("p (t n) -> p t n", t=TT)
        CB = flat(AUX[:, 16:22, :]).rearrange("p (g n) -> p g n", g=GROUPS)
        SEG = flat(AUX[:, 22:28, :]).rearrange("p (b n) -> p b n", n=WIDE)
        dt_, dtA, cum, dtx, dty, dtz, arow = (dts[:, i] for i in range(7))

        def bank(job):
            return PS[:, 4 + JOBS[job] % 4, :]

        def wait_made(e, job):
            n = JOBS[job]
            e.wait_ge(S(f"job_made{n % 4}"), n // 4 + 1)

        def made(ins, job):
            ins.then_inc(S(f"job_made{JOBS[job] % 4}"), 1)

        def wait_taken(e, job):
            n = JOBS[job]
            e.wait_ge(S(f"job_taken{n % 4}"), n // 4 + 1)

        def taken(ins, job):
            ins.then_inc(S(f"job_taken{JOBS[job] % 4}"), 1)

        def open_bank(e, job):
            n = JOBS[job]
            if n >= 4:
                e.wait_ge(S(f"job_taken{n % 4}"), n // 4)
            return PS[:, 4 + n % 4, :]

        def colt(name, t):
            return COLT0[name] + t

        def acc(n, c):
            return PS[:, 2 * (n % 2) + c, 0:TOK]

        def wait_column(e, name, t, groups=1):
            last = TILE0[name] + t * groups + groups - 1
            e.wait_ge(S(f"tile_used{last % SLOTS}"), last // SLOTS + 1)

        def evacuated(ins, name, t):
            ins.then_inc(S(f"pair_taken{colt(name, t) % 2}"), 1)

        def wait_evacuated(e, name, t):
            n = colt(name, t)
            e.wait_ge(S(f"pair_taken{n % 2}"), 2 * (n // 2 + 1))

        for s in range(SLOTS):
            S(f"tile_landed{s}"), S(f"tile_used{s}"), S(f"job_made{s}"), S(f"job_taken{s}")
        S("pair_taken0"), S("pair_taken1")

        class Steps:

            def __init__(self, eng, name):
                self.eng, self.sem, self.n = eng, S(name), 0

            def did(self, ins):
                ins.then_inc(self.sem, 1)
                self.n += 1

            def settle(self):
                self.eng.wait_ge(self.sem, self.n)

        UV = [flat(AUX[:, 8 * i:8 * i + 8, :]) for i in range(4)] + \
             [flat(CONV[:, 8 * i:8 * i + 8, :]) for i in range(3)] + [flat(V[:, :, :])]
        NB = len(UV)
        BODY = 2 * NB
        SPT = HEADS * TOPK
        NIT = SPT // BODY
        H2T = flat(PROJ[:, 0:8, :]).rearrange("p (t n) -> p t n", t=TT)
        YF = flat(PROJ[:, 8:16, :]).rearrange("p (t n) -> p t n", t=TT)
        QT = PROJ[:, 16:32, :]
        SCO = flat(PROJ[:, 32:48, :]).rearrange("p (t c n) -> p t c n", t=TT, c=16)
        CAND = flat(PROJ[:, 48:64, :]).rearrange("p (t n) -> p t n", t=TT)
        HOT = flat(PROJ[:, 64:72, :])
        HOT2 = flat(PROJ[:, 16:24, :])
        TV = SCR[:, 0:512].rearrange("p (t c k) -> p t c k", t=TT, c=16)
        TI = SCR[:, 512:1024].bitcast(U32).rearrange("p (t c k) -> p t c k", t=TT, c=16)
        TIF = SCR[:, 1024:1536].rearrange("p (t c k) -> p t c k", t=TT, c=16)
        TS = SCR[:, 1536:1792].rearrange("p (t h k) -> p t h k", t=TT, h=HEADS)
        TP = SCR[:, 1792:2048].bitcast(U32).rearrange("p (t h k) -> p t h k", t=TT, h=HEADS)
        TB = SCR[:, 2048:2304].bitcast(U32)
        TAF = SCR[:, 2304:2560].rearrange("p (t h k) -> p t h k", t=TT, h=HEADS)
        TBF = SCR[:, 2560:2816].rearrange("p (t h k) -> p t h k", t=TT, h=HEADS)
        EA = SCR[:, 2816:3072].rearrange("p (t n) -> p t n", t=TT)
        EB = SCR[:, 3072:3328].rearrange("p (t n) -> p t n", t=TT)
        EIDX = SCR[:, 3328:3584].bitcast(U32).rearrange("p (t n) -> p t n", t=TT)
        GT = SCR[:, 3584:3840].rearrange("p (t h k) -> p t h k", t=TT, h=HEADS)
        GS_ = small[:, 128:144]
        G16 = small[:, 160:176]
        DOT = small[:, 176:192]
        GEL = small[:, 192:208]
        W16 = small[:, 208:224]
        PRODS = [flat(PROJ[:, 48 + 4 * i:52 + 4 * i, :]) for i in range(2)]

        GATE, XR, XCV, RR, II, AA, T1, YR = (PROJ[:, 8 * i:8 * i + 8, :] for i in range(8))
        RGW = flat(CONV[:, 0:16, :]).rearrange("p (g n i m) -> p g n i m", g=2, n=8, i=2)
        HID = PROJ[:, 0:32, :]
        RL = [PROJ[:, 32 + i, :] for i in range(8)]
        SQ2 = PROJ[:, 64:72, :]
        BIAS = flat(CONV[:, :, :]).rearrange("p (h n) -> p h n", h=H_ATT)
        QT2, QI, KI, CR, CN = PROJ[:, 0:8, :], PROJ[:, 8:12, :], PROJ[:, 12, :], PROJ[:, 13, :], PROJ[:, 14, :]
        CTOK = PROJ[:, 15, :].rearrange("p (t c) -> p t c", t=TT)
        QLAT = PROJ[:, 16:32, :]
        w8 = flat(PROJ[:, 32:56, :]).rearrange("p (n k) -> p n k", k=WIDE)
        SCW, TMP, TMP2, MSK = w8[:, 0, :], w8[:, 1, :], w8[:, 2, :], w8[:, 3, :]
        PR = [w8[:, 4 + i, :] for i in range(4)]
        PT = [w8[:, 8 + i, :] for i in range(2)]
        OL = [w8[:, 10 + i, 0:TOK] for i in range(4)]
        OT = PROJ[:, 56:64, :]
        WI = small[:, 0:16].rearrange("p (t h) -> p t h", t=TT)
        BVS = AUX[0:16, 0:2, :].rearrange("p a b -> p (a b)")
        WWI = flat(AUX[:, 2:4, :])[:, 0:64].rearrange("p (k h) -> p k h", k=DC)
        SELH = flat(AUX[:, 4:6, :])[0:BUCKETS, 0:WIDE]
        RELB = flat(AUX[:, 6:8, :])[0:BUCKETS, 0:H_ATT]
        SK = flat(AUX[:, 28:30, :])[:, 0:2 * P].rearrange("p (j k) -> p j k", j=2)
        RGC = small[:, 16:32]
        MX, SM = small[:, 32:64], small[:, 64:96]

        def SQA(h):
            return PROJ[:, 8 + h, :]

        ukuv = ring[:, (TILE0["uk_uv"]) % SLOTS, :]
        UK = ukuv[:, 0:1024].rearrange("p (g c) -> p g c", g=8)
        UVV = ukuv[:, 1024:2048].rearrange("p (h v) -> p h v", h=H_ATT)

        block = ctx.enter_context(nc.Block())

        @block.sync
        def _(sp):
            def load(i, s):
                sp.dma_start(ring[:, s, :], io["stream"][SLOTS * i + s]).then_inc(S(f"tile_landed{s}"), 16)

            sp.dma_start(par[:, :], io["par"]).then_inc(S("params_landed"), 16)
            sp.dma_start(con[:, :], io["con"]).then_inc(S("params_landed"), 16)
            sp.dma_start(X[:, :, :], io["xT"]).then_inc(S("x_landed"), 16)
            sp.wait_ge(S("ada_landed3"), 32)
            for s in range(SLOTS):
                load(0, s)
            with sp.Fori(1, N_TILES // SLOTS) as i:
                for s in range(SLOTS):
                    sp.wait_ge(S(f"tile_used{s}"), i)
                    sp.dma_start(ring[:, s, :], io["stream"][bass.ds(SLOTS * i + s, 1)]
                                 .rearrange("o p n -> p (o n)")).then_inc(S(f"tile_landed{s}"), 16)
            sp.wait_ge(S("out_ready"), DC)
            sp.dma_start(io["outT"], H[:, :, :]).then_inc(S("out_stored"), 16)
            sp.wait_ge(S("out_stored"), 16)

        @block.tensor
        def _(pe):
            def tile_wait(name, i):
                t = TILE0[name] + i
                pe.wait_ge(S(f"tile_landed{t % SLOTS}"), 16 * (t // SLOTS + 1))
                return ring[:, t % SLOTS, :].rearrange("p (k n) -> p k n", k=DC)

            def tile_done(ins, name, i):
                ins.then_inc(S(f"tile_used{(TILE0[name] + i) % SLOTS}"), 1)

            def project(name, t, src, groups=1):
                n = colt(name, t)
                if n >= 2:
                    pe.wait_ge(S(f"pair_taken{n % 2}"), 2 * (n // 2))
                for g in range(groups):
                    w = tile_wait(name, t * groups + g)
                    for c in range(2):
                        for k in range(DC):
                            mm = pe.matmul(acc(n, c), w[:, k, c * P:(c + 1) * P], src[:, g * DC + k, :],
                                           start=(g == 0 and k == 0), stop=(g == groups - 1 and k == DC - 1))
                    tile_done(mm, name, t * groups + g)

            def sum_chunks(job, src, n, width=TOK):
                o = open_bank(pe, job)
                for k in range(n):
                    mm = pe.matmul(o[:, 0:width], ones, src[:, k, :], start=(k == 0), stop=(k == n - 1))
                made(mm, job)

            pe.wait_ge(S("params_landed"), 32)

            o = open_bank(pe, "mod_a")
            pe.wait_ge(S("ada_tiles"), 8 * DC)
            for i in range(8):
                for c in range(2):
                    mm = pe.matmul(o[:, 2 * i + c:2 * i + c + 1], CONV[:, 16 + i, c * P:(c + 1) * P], ones[:, 0:1],
                                   start=(i + c == 0), stop=True, skip_group_check=True)
            made(mm, "mod_a")

            pe.wait_ge(S("h_ready"), DC)
            for t in range(4):
                project("q", t, H)
            for t in range(4):
                project("k", t, H)
            for t in range(4):
                n = colt("v", t)
                pe.wait_ge(S(f"pair_taken{n % 2}"), 2 * (n // 2))
                w = tile_wait("v", t)
                for c in range(TT):
                    for k in range(DC):
                        mm = pe.matmul(acc(n, c), H[:, k, c * P:(c + 1) * P], w[:, k, :], start=(k == 0), stop=(k == DC - 1))
                tile_done(mm, "v", t)

            def scores(h):
                for j in range(2):
                    o = open_bank(pe, ("s", h, j))
                    q, k = Q[64 * j:64 * j + 64, h, :], K[64 * j:64 * j + 64, h, :]
                    pe.matmul(o[:, 0:P], q[:, 0:P], k[:, 0:P], start=True, stop=True)
                    mm = pe.matmul(o[:, P:WIDE], q[:, P:TOK], k[:, :], start=True, stop=True)
                    made(mm, ("s", h, j))

            def attend_transpose(h):
                o = open_bank(pe, ("t", h))
                pe.wait_ge(S("da_diff"), h + 1)
                a = AM[h % 2]
                pe.transpose(o[:, 0:P], a[:, 0:P], ident)
                pe.transpose(o[:, P:2 * P], a[:, P:2 * P], ident)
                made(pe.transpose(o[:, 2 * P:3 * P], a[:, 2 * P:3 * P], ident), ("t", h))

            def attend(h):
                o = open_bank(pe, ("o", h))
                wait_taken(pe, ("t", h))
                at = AT[h % 2]
                pe.matmul(o[:, 0:TOK], V[:, 0, h * P:(h + 1) * P], at[:, 0:TOK], start=True, stop=False)
                made(pe.matmul(o[:, P:TOK], V[:, 1, h * P:(h + 1) * P], at[:, TOK:WIDE], start=False, stop=True), ("o", h))

            wait_evacuated(pe, "k", 3)
            wait_evacuated(pe, "k", 2)
            scores(0)
            rest = [("xbc", t) for t in range(12)] + [("z", t) for t in range(8)] + [("g", t) for t in range(8)]
            for h in range(HEADS):
                if h == 1:
                    o = open_bank(pe, "dt")
                    pe.wait_ge(S("wdt_landed"), 16)
                    for t in range(TT):
                        for k in range(DC):
                            mm = pe.matmul(o[:, 32 * t:32 * t + 32], H[:, k, t * P:(t + 1) * P], wdt[:, k, :],
                                           start=(k == 0), stop=(k == DC - 1))
                    made(mm, "dt")
                if h == 4:
                    o = open_bank(pe, "mod_b")
                    pe.wait_ge(S("ada_tiles"), 24 * DC)
                    for i in range(16):
                        for c in range(2):
                            mm = pe.matmul(o[:, 2 * i + c:2 * i + c + 1], CONV[:, i, c * P:(c + 1) * P], ones[:, 0:1],
                                           start=(i + c == 0), stop=True, skip_group_check=True)
                    made(mm, "mod_b")
                    pe.wait_ge(S("dta_ready"), 1)
                    o = open_bank(pe, "cum0")
                    made(pe.matmul(o[:, 0:32], cst("triu", 0, P), dtA[:, 0, :], start=True, stop=True), "cum0")
                    o = open_bank(pe, "cum1")
                    pe.matmul(o[:, 0:32], ones, dtA[:, 0, :], start=True, stop=False)
                    made(pe.matmul(o[:, 0:32], cst("triu", 0, P), dtA[:, 1, :], start=False, stop=True), "cum1")
                for name, t in rest[4 * h:4 * h + 4]:
                    project(name, t, H)
                attend_transpose(h)
                if h + 1 < HEADS:
                    scores(h + 1)
                if h == 0:
                    wait_evacuated(pe, "v", 2)
                    wait_evacuated(pe, "v", 3)
                attend(h)
            for h in range(HEADS):
                o = open_bank(pe, ("yn", h))
                pe.wait_ge(S("da_square"), h + 1)
                made(pe.matmul(o[:, 0:TOK], ones, SQA(h), start=True, stop=True), ("yn", h))

            pe.wait_ge(S("conv_ready"), 24)
            for i in range(8):
                o = open_bank(pe, ("xs", i))
                t, q = i % 2, i // 2
                for c in range(4):
                    mm = pe.transpose(o[:, c * P:(c + 1) * P], CONV[:, 4 * q + c, t * P:(t + 1) * P], ident)
                made(mm, ("xs", i))
            for g in range(GROUPS):
                o = open_bank(pe, ("cb", g))
                b, c = CONV[:, 16 + g, :], CONV[:, 20 + g, :]
                pe.matmul(o[:, 0:TOK], b[:, 0:P], c, start=True, stop=True)
                made(pe.matmul(o[:, TOK:WIDE], b[:, P:TOK], c[:, P:TOK], start=True, stop=True), ("cb", g))

            def cum_row(h):
                o = open_bank(pe, ("cr", h))
                pe.matmul(o[:, 0:TOK], dtA[:, 0, h:h + 1].broadcast_to([P, P]), cst("triu"), start=True, stop=False)
                made(pe.matmul(o[:, P:TOK], dtA[:, 1, h:h + 1].broadcast_to([P, P]), cst("triu", 0, P),
                               start=False, stop=True), ("cr", h))

            cum_row(0)
            cum_row(1)
            for pair in range(SSD_HEADS // 2):
                if pair + 1 < SSD_HEADS // 2:
                    cum_row(2 * pair + 2)
                    cum_row(2 * pair + 3)
                o = open_bank(pe, ("y", pair))
                if pair == 0:
                    for i in (4, 5, 6, 7):
                        wait_taken(pe, ("xs", i))
                for e in range(2):
                    h = 2 * pair + e
                    pe.wait_ge(S("ssd_w"), h + 1)
                    w = SEG[:, h % 4, :]
                    y = o[64 * e:64 * e + 64, :]
                    pe.matmul(y[:, 0:TOK], XDT[:, 0, 64 * h:64 * h + 64], w[:, 0:TOK], start=True, stop=False)
                    mm = pe.matmul(y[:, P:TOK], XDT[:, 1, 64 * h:64 * h + 64], w[:, TOK:WIDE], start=False, stop=True)
                made(mm, ("y", pair))
            pe.wait_ge(S("ya_ready"), 1)
            for t in range(4):
                project("attn", t, YA)
            for g in range(GROUPS):
                pe.wait_ge(S("ys_square"), 4 * (g + 1))
                sum_chunks(("gn", g), CONV[:, 4 * g:4 * g + 4, :], 4)
            pe.wait_ge(S("ys_ready"), 16)
            for t in range(4):
                project("ssd", t, YS, 2)
            wait_evacuated(pe, "ssd", 2)
            wait_evacuated(pe, "ssd", 3)
            for t in range(4):
                project("out", t, MIX)

            wait_evacuated(pe, "out", 2)
            wait_evacuated(pe, "out", 3)
            sum_chunks("mean1", X, DC)
            pe.wait_ge(S("ln_square"), 1)
            sum_chunks("var1", PROJ[:, 48:56, :], DC)

            pe.wait_ge(S("h_ready"), 2 * DC)
            for i in range(4):
                o = open_bank(pe, ("h2", i))
                t, q = i // 2, i % 2
                for c in range(4):
                    mm = pe.transpose(o[:, c * P:(c + 1) * P], H[:, 4 * q + c, t * P:(t + 1) * P], ident)
                made(mm, ("h2", i))

            def key_scores(t):
                wait_evacuated(pe, "query", t)
                for c in (2 * t, 2 * t + 1):
                    o = open_bank(pe, ("sc", c))
                    for u in range(TT):
                        mm = pe.matmul(o[:, u * P:(u + 1) * P], QT[:, c, u * P:(u + 1) * P], SK[:, c % 2, :],
                                       start=True, stop=True)
                    made(mm, ("sc", c))

            pe.wait_ge(S("sk_landed"), 16)
            for t in range(8):
                project("query", t, H)
                if t:
                    key_scores(t - 1)
            key_scores(7)

            pe.wait_ge(S("uv_used7"), 2 * 2 * NIT)
            for i in range(4):
                o = open_bank(pe, ("yt", i))
                for c in range(2):
                    for t in range(TT):
                        mm = pe.transpose(o[:, c * TOK + t * P:c * TOK + (t + 1) * P],
                                          YF[:, t, (2 * i + c) * P:(2 * i + c + 1) * P], ident)
                made(mm, ("yt", i))
            for i in range(4):
                wait_taken(pe, ("yt", i))
            sum_chunks("mean2", X, DC)
            pe.wait_ge(S("ln_square"), 2)
            sum_chunks("var2", PROJ[:, 48:56, :], DC)

            def rms(job, k):
                pe.wait_ge(S("rms_square"), k)
                sum_chunks(job, SQ2, DC)

            rms("rms_mix0", 1)
            pe.wait_ge(S("h_ready"), 3 * DC)
            for t in range(8):
                project("rec_in", t, H)
            pe.wait_ge(S("rgw_landed"), 16)
            pe.wait_ge(S("xcv_sum"), DC)
            for c in range(DC):
                o = open_bank(pe, ("rg", c))
                n, oc = c // 2, c % 2
                for g in range(2):
                    for k in range(2):
                        mm = pe.matmul(o[:, g * TOK:(g + 1) * TOK], RGW[:, g, 2 * n + k, oc, :], XCV[:, 2 * n + k, :],
                                       start=(k == 0), stop=(k == 1))
                made(mm, ("rg", c))
            pe.wait_ge(S("yr_ready"), 1)
            for t in range(4):
                project("rec_out", t, YR)

            def mlp(layer):
                up, down = f"up{layer}", f"down{layer}"
                n0, t0 = COLT0[up], TILE0[up]
                with pe.Fori(0, 4) as i:
                    for s in range(4):
                        n = n0 + s
                        pe.wait_ge(S(f"pair_taken{n % 2}"), 2 * (n // 2) + i * 4)
                        pe.wait_ge(S(f"tile_landed{(t0 + s) % SLOTS}"), 16 * ((t0 + s) // SLOTS + 1) + i * 16)
                        w = ring[:, (t0 + s) % SLOTS, :].rearrange("p (k n) -> p k n", k=DC)
                        for c in range(2):
                            for k in range(DC):
                                mm = pe.matmul(acc(n, c), w[:, k, c * P:(c + 1) * P], H[:, k, :],
                                               start=(k == 0), stop=(k == DC - 1))
                        mm.then_inc(S(f"tile_used{(t0 + s) % SLOTS}"), 1)
                pe.wait_ge(S("hidden"), 32 * (layer + 1) + 1)
                n0, t0 = COLT0[down], TILE0[down]
                with pe.Fori(0, 2) as i:
                    for half in range(2):
                        n = n0 + half
                        pe.wait_ge(S(f"pair_taken{n % 2}"), 2 * (n // 2) + i * 2)
                        for g in range(4):
                            s = t0 + 4 * half + g
                            pe.wait_ge(S(f"tile_landed{s % SLOTS}"), 16 * (s // SLOTS + 1) + i * 32)
                            w = ring[:, s % SLOTS, :].rearrange("p (k n) -> p k n", k=DC)
                            for c in range(2):
                                for k in range(DC):
                                    mm = pe.matmul(acc(n, c), w[:, k, c * P:(c + 1) * P], HID[:, g * DC + k, :],
                                                   start=(g == 0 and k == 0), stop=(g == 3 and k == DC - 1))
                            mm.then_inc(S(f"tile_used{s % SLOTS}"), 1)

            rms("rms_mlp0", 2)
            pe.wait_ge(S("h_ready"), 4 * DC)
            mlp(0)

            o = open_bank(pe, "bv")
            pe.wait_ge(S("bias_consts_landed"), 48)
            made(pe.matmul(o[0:16, 0:WIDE], RELB, SELH, start=True, stop=True), "bv")
            rms("rms_mix1", 3)
            pe.wait_ge(S("h_ready"), 5 * DC)
            for t in range(7):
                project("att_in", t, H)
            o = open_bank(pe, "wi")
            for t in range(TT):
                for k in range(DC):
                    mm = pe.matmul(o[:, 8 * t:8 * t + 8], H[:, k, t * P:(t + 1) * P], WWI[:, k, :],
                                   start=(k == 0), stop=(k == DC - 1))
            made(mm, "wi")
            o = open_bank(pe, "rms_c")
            pe.wait_ge(S("c_square"), 1)
            made(pe.matmul(o[:, 0:TOK], ones, TMP[:, 0:TOK], start=True, stop=True), "rms_c")
            o = open_bank(pe, "ctok")
            pe.wait_ge(S("cn_ready"), 1)
            pe.transpose(o[:, 0:P], CN[:, 0:P], ident)
            made(pe.transpose(o[:, P:TOK], CN[:, P:TOK], ident), "ctok")
            wait_evacuated(pe, "att_in", 6)
            for h in range(H_IDX):
                o = open_bank(pe, ("dot", h))
                a, b = 64 * (h % 2), 64 * (h % 2) + 64
                pe.matmul(o[:, 0:P], QI[a:b, h // 2, 0:P], KI[a:b, 0:P], start=True, stop=True)
                made(pe.matmul(o[:, P:WIDE], QI[a:b, h // 2, P:TOK], KI[a:b, :], start=True, stop=True), ("dot", h))
            s = TILE0["uk_uv"]
            pe.wait_ge(S(f"tile_landed{s % SLOTS}"), 16 * (s // SLOTS + 1))
            for h in range(H_ATT):
                o = open_bank(pe, ("ql", h))
                a, b = 64 * (h % 2), 64 * (h % 2) + 64
                made(pe.matmul(o[:, 0:TOK], UK[a:b, h // 2, :], QT2[a:b, h // 2, :], start=True, stop=True), ("ql", h))

            def logits(h):
                o = open_bank(pe, ("lg", h))
                if h == 0:
                    pe.wait_ge(S("bias_landed"), 32)
                    for i in range(12, 16):
                        wait_taken(pe, ("ql", i))
                pe.matmul(o[:, 0:WIDE], cst("flip"), BIAS[:, h, :], start=True, stop=False)
                pe.matmul(o[:, 0:P], QLAT[:, h, 0:P], CN[:, 0:P], start=False, stop=False)
                made(pe.matmul(o[:, P:WIDE], QLAT[:, h, P:TOK], CN, start=False, stop=True), ("lg", h))

            logits(0)
            logits(1)
            for h in range(H_ATT):
                if h + 2 < H_ATT:
                    logits(h + 2)
                o = open_bank(pe, ("pt", h))
                pe.wait_ge(S("p_ready"), h + 1)
                p = PR[h % 4]
                pe.transpose(o[:, 0:P], p[:, 0:P], ident)
                pe.transpose(o[:, P:2 * P], p[:, P:2 * P], ident)
                made(pe.transpose(o[:, 2 * P:3 * P], p[:, 2 * P:3 * P], ident), ("pt", h))
                o = open_bank(pe, ("ol", h))
                wait_taken(pe, ("pt", h))
                pt = PT[h % 2]
                pe.matmul(o[:, 0:TOK], CTOK[:, 0, :], pt[:, 0:TOK], start=True, stop=False)
                made(pe.matmul(o[:, P:TOK], CTOK[:, 1, :], pt[:, TOK:WIDE], start=False, stop=True), ("ol", h))
                if h % 2 == 1:
                    o = open_bank(pe, ("ot", h // 2))
                    for e in range(2):
                        wait_taken(pe, ("ol", h - 1 + e))
                        mm = pe.matmul(o[64 * e:64 * e + 64, 0:TOK], UVV[:, h - 1 + e, :], OL[(h - 1 + e) % 4],
                                       start=True, stop=True)
                    if h < H_ATT - 1:
                        made(mm, ("ot", h // 2))
                    else:
                        made(mm, ("ot", h // 2))
                        pe.wait_ge(S(f"job_made{JOBS[('ot', 7)] % 4}"), JOBS[("ot", 7)] // 4 + 1)
                        pe.sem_inc(S(f"tile_used{TILE0['uk_uv'] % SLOTS}"), 1)
            for g in range(4):
                wait_taken(pe, ("ot", 4 + g))
            for t in range(4):
                project("att_out", t, OT)
            rms("rms_mlp1", 4)
            pe.wait_ge(S("h_ready"), 6 * DC)
            mlp(1)
            rms("rms_fin", 5)

        @block.gpsimd
        def _(pool):
            pool.wait_ge(S("params_landed"), 32)
            for h in range(HEADS):
                slope = 2.0 ** (-8.0 * (h + 1) / HEADS)
                if h >= 2:
                    wait_taken(pool, ("s", h - 2, 1))
                pool.tensor_scalar(AB[h % 2], cst("dist"), -slope / DA_SCALE, 1.0, ALU.mult, ALU.mult)\
                    .then_inc(S("da_bias"), 1)

            pool.wait_ge(S("experts_ready"), 1)
            for n in range(TT * SPT):
                b = n % NB
                if n >= NB:
                    pool.wait_ge(S(f"uv_used{b}"), n // NB)
                pool.indirect_dma_start(
                    out=UV[b], out_offset=None, in_=io["peer_uv"],
                    in_offset=bass.IndirectOffsetOnAxis(ap=EIDX[:, n // SPT, n % SPT:n % SPT + 1], axis=0),
                ).then_inc(S(f"uv_landed{b}"), 16)

        @block.scalar
        def _(act):
            st = Steps(act, "act_step")

            def on(*a, **k):
                st.did(act.activation(*a, **k))

            act.dma_start(rows[:, :], io["rows"]).then_inc(S("rows_landed"), 16)
            for s in range(SLOTS):
                act.dma_start(flat(adaW[:, s]), io["ada"][s]).then_inc(S(f"ada_landed{s}"), 16)
            act.dma_start(wdt[:, :, :], io["wdt"]).then_inc(S("wdt_landed"), 16)
            act.wait_ge(S("params_landed"), 32)
            act.activation(small[:, 240:248], pc("c", 0, 8), ACT.Silu).then_inc(S("c_ready"), 1)

            def ada_load(i):
                for s in range(SLOTS):
                    act.wait_ge(S("ada_tiles"), (i - 1) * 4 * DC + 4 * (DC - 1) + s + 1)
                    act.dma_start(flat(adaW[:, s]), io["ada"][4 * i + s]).then_inc(S(f"ada_landed{s}"), 16)

            ada_load(1)
            ada_load(2)
            act.wait_ge(S("h_ready"), DC)
            act.activation(X[:, :, :], X[:, :, :], ACT.Copy, scale=ALPHA).then_inc(S("x_scaled"), 1)
            act.wait_ge(S("lam_dots"), 2)
            act.activation(small[:, 18:20], small[:, 16:18], ACT.Exp).then_inc(S("lam_exp"), 1)

            def copy_out(name, t, dst):
                n = colt(name, t)
                wait_column(act, name, t)
                for c in range(2):
                    evacuated(act.activation(dst(c), acc(n, c), ACT.Copy), name, t)

            for t in range(4):
                copy_out("q", t, lambda c: Q[:, 2 * t + c, :])
            for t in range(4):
                copy_out("k", t, lambda c: K[:, 2 * t + c, :])
            for t in range(4):
                copy_out("v", t, lambda c: V[:, c, COLS * t:COLS * (t + 1)])

            def da_exp(h):
                act.wait_ge(S("da_negmax"), h + 1)
                for j in range(2):
                    for t in range(TT):
                        k = 2 * j + t
                        s = SC[h % 2][j][:, 0:P] if t == 0 else SC[h % 2][j][:, P:WIDE]
                        act.activation(s, s, ACT.Exp, bias=small[:, 8 * (h % 2) + k:8 * (h % 2) + k + 1],
                                       accum_out=small[:, 8 * (h % 2) + 4 + k:8 * (h % 2) + 5 + k]).then_inc(S("da_exp"), 1)

            rest = [("xbc", t) for t in range(12)] + [("z", t) for t in range(8)] + [("g", t) for t in range(8)]
            dest = {"xbc": XBC, "z": Z, "g": G}
            for h in range(HEADS):
                da_exp(h)
                if h in (1, 2, 3):
                    ada_load(h + 2)
                for name, t in rest[4 * h:4 * h + 4]:
                    copy_out(name, t, lambda c: dest[name][:, 2 * t + c, :])
                wait_made(act, ("t", h))
                taken(act.activation(AT[h % 2], bank(("t", h))[:, 0:WIDE], ACT.Copy), ("t", h))
                wait_made(act, ("o", h))
                taken(act.activation(YA[:, h, :], bank(("o", h))[:, 0:TOK], ACT.Copy), ("o", h))
                if h == 2:
                    act.wait_ge(S("rows_landed"), 16)
                    on(arow[:, 0, :], row("a_log"), ACT.Exp)
                    act.wait_ge(S("dt_negabs"), 1)
                    on(flat(dty), flat(dtx), ACT.Exp)
                    st.settle()
                    act.activation(flat(dtz), flat(dty), ACT.Ln, bias=1.0).then_inc(S("dt_ln"), 1)
            for h in range(HEADS):
                if h == 0:
                    wait_taken(act, ("o", 7))
                    wait_taken(act, ("o", 6))
                act.activation(SQA(h), YA[:, h, :], ACT.Square).then_inc(S("da_square"), 1)
            for c in range(24):
                act.wait_ge(S("conv_sum"), c + 1)
                act.activation(CONV[:, c, :], CONV[:, c, :], ACT.Silu).then_inc(S("conv_ready"), 1)
            act.activation(Z[:, :, :], Z[:, :, :], ACT.Silu).then_inc(S("z_ready"), 1)
            act.activation(G[:, :, :], G[:, :, :], ACT.Sigmoid).then_inc(S("g_ready"), 1)
            act.wait_ge(S("da_var"), 1)
            act.activation(MIX[:, :, :], MIX[:, :, :], ACT.Sqrt).then_inc(S("da_rstd"), 1)
            for h in range(SSD_HEADS):
                wait_taken(act, ("cr", h))
                act.activation(SEG[:, h % 4, :], SEG[:, h % 4, :], ACT.Exp).then_inc(S("decay_ready"), 1)
            for c in range(16):
                act.wait_ge(S("ys_gated"), c + 1)
                act.activation(CONV[:, c, :], YS[:, c, :], ACT.Square).then_inc(S("ys_square"), 1)
            for g in range(GROUPS):
                act.wait_ge(S("gn_inv"), g + 1)
                act.activation(RS[:, :], RS[:, :], ACT.Sqrt).then_inc(S("gn_rstd"), 1)

            def norm_help(k):
                wait_taken(act, f"mean{k}")
                act.activation(PROJ[:, 48:56, :], H[:, :, :], ACT.Square).then_inc(S("ln_square"), 1)
                act.wait_ge(S("ln_inv"), k)
                act.activation(RS[:, :], RS[:, :], ACT.Sqrt).then_inc(S("ln_rstd"), 1)

            norm_help(1)
            act.wait_ge(S("ssd_w"), SSD_HEADS)
            act.dma_start(flat(SK), io["sk"]).then_inc(S("sk_landed"), 16)
            act.wait_ge(S("h_ready"), 2 * DC)
            act.activation(X[:, :, :], X[:, :, :], ACT.Copy, scale=ALPHA).then_inc(S("x_scaled"), 1)
            for i in range(4):
                wait_made(act, ("h2", i))
                t, q = i // 2, i % 2
                taken(act.activation(H2T[:, t, 512 * q:512 * q + 512], bank(("h2", i)), ACT.Copy), ("h2", i))

            def score_out(t):
                for c in (2 * t, 2 * t + 1):
                    wait_made(act, ("sc", c))
                    taken(act.activation(SCO[:, :, c, :], bank(("sc", c))[:, 0:TOK].rearrange("p (t n) -> p t n", t=TT),
                                         ACT.Copy), ("sc", c))

            for t in range(8):
                copy_out("query", t, lambda c: QT[:, 2 * t + c, :])
                if t:
                    score_out(t - 1)
            score_out(7)
            act.wait_ge(S("top_shifted"), 1)
            act.activation(GT[:, :, :, :].rearrange("p t h k -> p (t h k)"), EA[:, :, :].rearrange("p t n -> p (t n)"),
                           ACT.Exp).then_inc(S("top_exp"), 1)
            act.activation(GEL[:, 0:1], par[:, 0:1], ACT.Copy).then_inc(S("weight_ready"), 1)
            for tt in range(TT):
                with act.Fori(0, NIT) as i:
                    for k in range(BODY):
                        n = tt * SPT + k
                        act.wait_ge(S("dot_ready"), n + 1 + i * BODY)
                        act.activation(GEL[:, k:k + 1], DOT[:, k:k + 1], ACT.Gelu).then_inc(S("gelu_ready"), 1)
                        act.wait_ge(S("gelu_ready"), n + 1 + i * BODY)
                        act.activation(W16[:, k:k + 1], GEL[:, k:k + 1], ACT.Copy, scale=G16[:, k:k + 1])\
                            .then_inc(S("weight_ready"), 1)
            for b in range(NB):
                act.wait_ge(S(f"uv_used{b}"), 2 * 2 * NIT)
            act.dma_start(flat(CONV[:, 0:16, :]), io["rgw"]).then_inc(S("rgw_landed"), 16)
            act.dma_start(WWI[:, :, :], io["wwi"]).then_inc(S("bias_consts_landed"), 16)
            act.dma_start(SELH, io["selh"]).then_inc(S("bias_consts_landed"), 16)
            act.dma_start(RELB, io["relb"]).then_inc(S("bias_consts_landed"), 16)
            norm_help(2)

            def rms_help(k, last=None):
                if last:
                    wait_evacuated(act, last, 2)
                    wait_evacuated(act, last, 3)
                else:
                    act.wait_ge(S("x_ready"), DC)
                act.activation(SQ2[:, :, :], X[:, :, :], ACT.Square).then_inc(S("rms_square"), 1)
                act.wait_ge(S("rms_inv"), k)
                act.activation(RS[:, :], RS[:, :], ACT.Sqrt).then_inc(S("rms_rstd"), 1)

            act.wait_ge(S("lam_negabs"), 1)
            on(RGC[:, 8:16], RGC[:, 0:8], ACT.Exp)
            st.settle()
            act.activation(RGC[:, 0:8], RGC[:, 8:16], ACT.Ln, bias=1.0).then_inc(S("lam_ln"), 1)
            rms_help(1)
            for t in range(4):
                n = colt("rec_in", t)
                wait_column(act, "rec_in", t)
                for c in range(2):
                    evacuated(act.activation(GATE[:, 2 * t + c, :], acc(n, c), ACT.Gelu_apprx_tanh), "rec_in", t)
            for t in range(4, 8):
                copy_out("rec_in", t, lambda c: XR[:, 2 * (t - 4) + c, :])
            for c in range(DC):
                wait_made(act, ("rg", c))
                b = bank(("rg", c))
                on(RR[:, c, :], b[:, 0:TOK], ACT.Sigmoid, bias=pc("rec_b_a", c))
                taken(act.activation(II[:, c, :], b[:, TOK:2 * TOK], ACT.Sigmoid, bias=pc("rec_b_x", c)), ("rg", c))
            act.wait_ge(S("log_a"), DC)
            on(AA[:, :, :], RR[:, :, :], ACT.Exp)
            act.activation(RR[:, :, :], RR[:, :, :], ACT.Tanh).then_inc(S("a_ready"), 1)
            act.wait_ge(S("u_square"), 1)
            act.activation(T1[:, :, :], T1[:, :, :], ACT.Sqrt, scale=-1.0).then_inc(S("u_root"), 1)
            rms_help(2, "rec_out")

            def mlp(layer):
                up = f"up{layer}"
                n0, t0 = COLT0[up], TILE0[up]
                with act.Fori(0, 4) as i:
                    for s in range(4):
                        act.wait_ge(S(f"tile_used{(t0 + s) % SLOTS}"), (t0 + s) // SLOTS + 1 + i)
                        for c in range(2):
                            act.wait_ge(S("hidden"), 32 * layer + 1 + i * 8)
                            act.activation(RL[2 * s + c], acc(n0 + s, c), ACT.Relu)\
                                .then_inc(S(f"pair_taken{(n0 + s) % 2}"), 1)

            mlp(0)
            wait_made(act, "bv")
            taken(act.activation(BVS[:, 0:WIDE], bank("bv")[0:16, 0:WIDE], ACT.Copy), "bv")
            wait_taken(act, "bv")
            act.dma_start(io["bv"], BVS[:, 0:WIDE]).then_inc(S("bv_stored"), 16)
            act.wait_ge(S("bv_stored"), 16)
            bv = io["bv"]
            for q, a, b in ((0, 0, P), (1, P, WIDE)):
                src = bass.AP(tensor=bv.tensor, offset=bv.offset + P - P * q, ap=[[1, P], [WIDE, H_ATT], [1, b - a]])
                act.dma_start(BIAS[:, :, a:b], src).then_inc(S("bias_landed"), 16)
            rms_help(3, "down0")
            for t in range(4):
                copy_out("att_in", t, lambda c: QT2[:, 2 * t + c, :])
            copy_out("att_in", 4, lambda c: (CR, QI[:, 0, :])[c])
            copy_out("att_in", 5, lambda c: QI[:, 1 + c, :])
            wait_evacuated(act, "att_in", 4)
            act.activation(TMP[:, 0:TOK], CR, ACT.Square).then_inc(S("c_square"), 1)
            copy_out("att_in", 6, lambda c: (QI[:, 3, :], KI)[c])
            act.wait_ge(S("c_inv"), 1)
            act.activation(RS[:, :], RS[:, :], ACT.Sqrt).then_inc(S("c_rstd"), 1)
            wait_made(act, "ctok")
            taken(act.activation(CTOK[:, :, :], bank("ctok")[:, 0:TOK].rearrange("p (t c) -> p t c", t=TT), ACT.Copy), "ctok")
            for h in range(H_ATT):
                wait_made(act, ("ql", h))
                taken(act.activation(QLAT[:, h, :], bank(("ql", h))[:, 0:TOK], ACT.Copy, scale=ATT_SCALE), ("ql", h))

            def att_exp(h):
                act.wait_ge(S("lg_negmax"), h + 1)
                for t in range(TT):
                    p = PR[h % 4][:, 0:P] if t == 0 else PR[h % 4][:, P:WIDE]
                    k = 2 * (h % 4) + t
                    act.activation(p, p, ACT.Exp, bias=MX[:, k:k + 1], accum_out=SM[:, k:k + 1]).then_inc(S("lg_exp"), 1)

            att_exp(0)
            for h in range(H_ATT):
                if h + 1 < H_ATT:
                    att_exp(h + 1)
                wait_made(act, ("pt", h))
                taken(act.activation(PT[h % 2], bank(("pt", h))[:, 0:WIDE], ACT.Copy), ("pt", h))
                wait_made(act, ("ol", h))
                taken(act.activation(OL[h % 4], bank(("ol", h))[:, 0:TOK], ACT.Copy), ("ol", h))
                if h % 2 == 1:
                    wait_made(act, ("ot", h // 2))
                    taken(act.activation(OT[:, h // 2, :], bank(("ot", h // 2))[:, 0:TOK], ACT.Copy), ("ot", h // 2))
            rms_help(4, "att_out")
            mlp(1)
            rms_help(5, "down1")

        @block.vector
        def _(dve):
            st = Steps(dve, "dve_step")
            did, settle = st.did, st.settle
            cc = small[:, 240:248]

            def ada(i, base):
                for s in range(SLOTS):
                    dve.wait_ge(S(f"ada_landed{s}"), 16 * (i + 1))
                for k in range(DC):
                    for s in range(SLOTS):
                        o = CONV[:, base + s, :]
                        if k:
                            dve.wait_ge(S("ada_tiles"), 4 * DC * i + 4 * (k - 1) + s + 1)
                            ins = dve.scalar_tensor_tensor(o, adaW[:, s, k, :], cc[:, k:k + 1], o, ALU.mult, ALU.add)
                        else:
                            ins = dve.tensor_scalar(o, adaW[:, s, 0, :], cc[:, 0:1], None, ALU.mult)
                        ins.then_inc(S("ada_tiles"), 1)

            dve.wait_ge(S("c_ready"), 1)
            ada(0, 16)
            ada(1, 20)
            wait_made(dve, "mod_a")
            taken(dve.tensor_tensor(mod[:, 0:16], bank("mod_a")[:, 0:16], pc("b_ada", 0, 16), ALU.add), "mod_a")
            wait_taken(dve, "mod_a")
            did(dve.tensor_scalar(mod[:, 8:16], mod[:, 8:16], 1.0, None, ALU.add))
            settle()
            dve.wait_ge(S("x_landed"), 16)
            for c in range(DC):
                dve.tensor_scalar(H[:, c, :], X[:, c, :], mod[:, 8 + c:9 + c], mod[:, c:c + 1], ALU.mult, ALU.add)\
                    .then_inc(S("h_ready"), 1)
            dve.wait_ge(S("rows_landed"), 16)
            for i in (1, 2):
                q, k = row(f"lambda_q{i}"), row(f"lambda_k{i}")
                dve.tensor_tensor_reduce(q, q, k, 1.0, 0.0, ALU.mult, ALU.add, small[:, 15 + i:16 + i])\
                    .then_inc(S("lam_dots"), 1)

            def da_scores(h):
                dve.wait_ge(S("da_bias"), h + 1)
                m = small[:, 8 * (h % 2):8 * (h % 2) + 4]
                for j in range(2):
                    wait_made(dve, ("s", h, j))
                    b = bank(("s", h, j))
                    if j == 0 and h >= 2:
                        dve.wait_ge(S("da_diff"), h - 1)
                    for t, (x, y) in enumerate(((0, P), (P, WIDE))):
                        ins = dve.tensor_tensor_reduce(SC[h % 2][j][:, x:y], b[:, x:y], AB[h % 2][:, x:y], DA_SCALE, NEG,
                                                       ALU.add, ALU.max, m[:, 2 * j + t:2 * j + t + 1])
                        if t:
                            taken(ins, ("s", h, j))
                        else:
                            did(ins)
                wait_taken(dve, ("s", h, 0))
                wait_taken(dve, ("s", h, 1))
                dve.tensor_scalar(m, m, -1.0, None, ALU.mult).then_inc(S("da_negmax"), 1)

            def da_combine(h):
                dve.wait_ge(S("da_exp"), 4 * (h + 1))
                sums = small[:, 8 * (h % 2) + 4:8 * (h % 2) + 8]
                did(dve.reciprocal(sums, sums))
                settle()
                did(dve.tensor_scalar(sums[:, 2:4], sums[:, 2:4], small[:, 20:21], None, ALU.mult))
                settle()
                if h >= 2:
                    wait_made(dve, ("t", h - 2))
                for t, (x, y) in enumerate(((0, P), (P, WIDE))):
                    did(dve.tensor_scalar(AM[h % 2][:, x:y], SC[h % 2][0][:, x:y], sums[:, t:t + 1], None, ALU.mult))
                settle()
                for t, (x, y) in enumerate(((0, P), (P, WIDE))):
                    ins = dve.scalar_tensor_tensor(AM[h % 2][:, x:y], SC[h % 2][1][:, x:y], sums[:, 2 + t:3 + t],
                                                   AM[h % 2][:, x:y], ALU.mult, ALU.add)
                    if t:
                        ins.then_inc(S("da_diff"), 1)
                    else:
                        did(ins)

            def conv(c0, n, src, w, b, chunks, dst, sem):
                for k in (3, 2, 1, 0):
                    d = 3 - k
                    if d:
                        settle()
                    for c in range(c0, c0 + n):
                        o, x, wk = dst[:, c, :], src[:, c, :], pc(w, k * chunks + c)
                        if d == 0:
                            did(dve.tensor_scalar(o, x, wk, pc(b, c), ALU.mult, ALU.add))
                            continue
                        ins = dve.scalar_tensor_tensor(o[:, d:TOK], x[:, 0:TOK - d], wk, o[:, d:TOK], ALU.mult, ALU.add)
                        if k:
                            did(ins)
                        else:
                            ins.then_inc(S(sem), 1)

            for h in range(HEADS):
                da_scores(h)
                if h == 0:
                    dve.wait_ge(S("lam_exp"), 1)
                    did(dve.scalar_tensor_tensor(small[:, 20:21], small[:, 19:20], -LAMBDA_INIT, small[:, 18:19],
                                                 ALU.add, ALU.subtract))
                    settle()
                if h == 1:
                    dve.wait_ge(S("rows_landed"), 16)
                    wait_made(dve, "dt")
                    taken(dve.tensor_tensor(dt_[:, :, :], bank("dt")[:, 0:64].rearrange("p (t n) -> p t n", t=TT),
                                            over(row("dt_bias"), TT), ALU.add), "dt")
                    wait_taken(dve, "dt")
                    dve.scalar_tensor_tensor(flat(dtx), flat(dt_), -1.0, flat(dt_), ALU.mult, ALU.min).then_inc(S("dt_negabs"), 1)
                if h < 4:
                    ada(2 + h, 4 * h)
                da_combine(h)
                if h == 3:
                    dve.wait_ge(S("dt_ln"), 1)
                    did(dve.scalar_tensor_tensor(flat(dt_), flat(dt_), 0.0, flat(dtz), ALU.max, ALU.add))
                    settle()
                    dve.scalar_tensor_tensor(dtA[:, :, :], dt_[:, :, :], -1.0, over(arow[:, 0, :], TT), ALU.mult, ALU.mult)\
                        .then_inc(S("dta_ready"), 1)
                if h == 4:
                    wait_made(dve, "mod_b")
                    taken(dve.tensor_tensor(mod[:, 16:48], bank("mod_b")[:, 0:32], pc("b_ada", 16, 32), ALU.add), "mod_b")
                    wait_taken(dve, "mod_b")
                    did(dve.tensor_scalar(mod[:, 32:40], mod[:, 32:40], 1.0, None, ALU.add))
                    for t in range(TT):
                        wait_made(dve, f"cum{t}")
                        taken(dve.tensor_copy(cum[:, t, :], bank(f"cum{t}")[:, 0:32]), f"cum{t}")
                        wait_taken(dve, f"cum{t}")
                if 4 <= h < 7:
                    for t in range(4 * (h - 4), 4 * (h - 4) + 4):
                        wait_evacuated(dve, "xbc", t)
                    conv(8 * (h - 4), 8, XBC, "conv_w", "conv_b", 24, CONV, "conv_sum")

            for h in range(HEADS):
                wait_made(dve, ("yn", h))
                taken(dve.tensor_scalar(MIX[:, h, :], bank(("yn", h))[:, 0:TOK], 1.0 / P, EPS, ALU.mult, ALU.add), ("yn", h))
            for h in range(4, 8):
                wait_taken(dve, ("yn", h))
            dve.reciprocal(MIX[:, :, :], MIX[:, :, :]).then_inc(S("da_var"), 1)
            did(dve.tensor_scalar(small[:, 21:22], pc("subln"), 1.0 - LAMBDA_INIT, None, ALU.mult))
            for i in range(8):
                wait_made(dve, ("xs", i))
                t, q = i % 2, i // 2
                taken(dve.tensor_tensor(XDT[:, t, 512 * q:512 * q + 512].rearrange("p (h n) -> p h n", n=64),
                                        bank(("xs", i)).rearrange("p (h n) -> p h n", n=64),
                                        dt_[:, t, 8 * q:8 * q + 8].rearrange("p (h o) -> p h o", o=1).broadcast_to([P, 8, 64]),
                                        ALU.mult), ("xs", i))
            for g in range(GROUPS):
                wait_made(dve, ("cb", g))
                b = bank(("cb", g))
                did(dve.tensor_tensor(CB[:, g, 0:TOK], b[:, 0:TOK], cst("triu"), ALU.mult))
                taken(dve.tensor_tensor(CB[:, g, TOK:WIDE], b[:, TOK:WIDE], cst("triu", 0, P), ALU.mult), ("cb", g))
            settle()
            for g in range(GROUPS):
                wait_taken(dve, ("cb", g))
            dve.wait_ge(S("da_rstd"), 1)
            dve.scalar_tensor_tensor(YA[:, :, :], YA[:, :, :], small[:, 21:22], MIX[:, :, :], ALU.mult, ALU.mult)\
                .then_inc(S("ya_ready"), 1)

            def segment(h):
                wait_made(dve, ("cr", h))
                b = bank(("cr", h))
                if h >= 4:
                    wait_made(dve, ("y", (h - 4) // 2))
                did(dve.tensor_scalar(SEG[:, h % 4, 0:TOK], b[:, 0:TOK], cum[:, 0, h:h + 1], 0.0, ALU.subtract, ALU.min))
                taken(dve.tensor_scalar(SEG[:, h % 4, TOK:WIDE], b[:, P:TOK], cum[:, 1, h:h + 1], 0.0,
                                        ALU.subtract, ALU.min), ("cr", h))

            def weigh(h):
                dve.wait_ge(S("decay_ready"), h + 1)
                dve.tensor_tensor(SEG[:, h % 4, :], SEG[:, h % 4, :], CB[:, h // 8, :], ALU.mult).then_inc(S("ssd_w"), 1)

            def gate_out(pair):
                wait_made(dve, ("y", pair))
                taken(dve.scalar_tensor_tensor(YS[:, pair, :], CONV[:, pair, :], pc("d_skip", pair), bank(("y", pair))[:, 0:TOK],
                                               ALU.mult, ALU.add), ("y", pair))
                wait_taken(dve, ("y", pair))
                if pair == 0:
                    dve.wait_ge(S("z_ready"), 1)
                dve.tensor_tensor(YS[:, pair, :], YS[:, pair, :], Z[:, pair, :], ALU.mult).then_inc(S("ys_gated"), 1)

            segment(0)
            segment(1)
            for pair in range(SSD_HEADS // 2):
                if pair >= 1:
                    gate_out(pair - 1)
                if pair + 1 < SSD_HEADS // 2:
                    segment(2 * pair + 2)
                weigh(2 * pair)
                if pair + 1 < SSD_HEADS // 2:
                    segment(2 * pair + 3)
                weigh(2 * pair + 1)
            gate_out(SSD_HEADS // 2 - 1)

            dve.wait_ge(S("g_ready"), 1)
            for t in range(4):
                n = colt("attn", t)
                wait_column(dve, "attn", t)
                for c in range(2):
                    k = 2 * t + c
                    evacuated(dve.tensor_tensor(MIX[:, k, :], acc(n, c), G[:, k, :], ALU.mult), "attn", t)
            for g in range(GROUPS):
                wait_made(dve, ("gn", g))
                taken(dve.tensor_scalar(RS[:, :], bank(("gn", g))[:, 0:TOK], 1.0 / 512, EPS, ALU.mult, ALU.add), ("gn", g))
                wait_taken(dve, ("gn", g))
                dve.reciprocal(RS[:, :], RS[:, :]).then_inc(S("gn_inv"), 1)
                dve.wait_ge(S("gn_rstd"), g + 1)
                for k in range(4 * g, 4 * g + 4):
                    dve.scalar_tensor_tensor(YS[:, k, :], YS[:, k, :], pc("ssd_norm_w", k), RS[:, :], ALU.mult, ALU.mult)\
                        .then_inc(S("ys_ready"), 1)
                dve.wait_ge(S("ys_ready"), 4 * (g + 1))
            for t in range(4):
                n = colt("ssd", t)
                wait_column(dve, "ssd", t, 2)
                for c in range(2):
                    k = 2 * t + c
                    did(dve.tensor_tensor(G[:, k, :], acc(n, c), G[:, 8 + k, :], ALU.mult))
                settle()
                for c in range(2):
                    k = 2 * t + c
                    evacuated(dve.tensor_tensor(MIX[:, k, :], MIX[:, k, :], G[:, k, :], ALU.add), "ssd", t)
            dve.wait_ge(S("x_scaled"), 1)
            for t in range(4):
                n = colt("out", t)
                wait_column(dve, "out", t)
                for c in range(2):
                    k = 2 * t + c
                    evacuated(dve.scalar_tensor_tensor(X[:, k, :], acc(n, c), mod[:, 16 + k:17 + k], X[:, k, :],
                                                       ALU.mult, ALU.add), "out", t)

            def layer_norm(i, g, b):
                wait_made(dve, f"mean{i}")
                taken(dve.scalar_tensor_tensor(H[:, :, :], over(bank(f"mean{i}")[:, 0:TOK], DC), -1.0 / D, X[:, :, :],
                                               ALU.mult, ALU.add), f"mean{i}")
                wait_made(dve, f"var{i}")
                taken(dve.tensor_scalar(RS[:, :], bank(f"var{i}")[:, 0:TOK], 1.0 / D, EPS, ALU.mult, ALU.add), f"var{i}")
                wait_taken(dve, f"var{i}")
                dve.reciprocal(RS[:, :], RS[:, :]).then_inc(S("ln_inv"), 1)
                dve.wait_ge(S("ln_rstd"), i)
                for c in range(DC):
                    did(dve.scalar_tensor_tensor(X[:, c, :], H[:, c, :], pc(g, c), RS[:, :], ALU.mult, ALU.mult))
                settle()

            layer_norm(1, "ln1_g", "ln1_b")
            for c in range(DC):
                did(dve.tensor_scalar(X[:, c, :], X[:, c, :], pc("ln1_b", c), None, ALU.add))
            settle()
            for c in range(DC):
                dve.tensor_scalar(H[:, c, :], X[:, c, :], mod[:, 32 + c:33 + c], mod[:, 24 + c:25 + c], ALU.mult, ALU.add)\
                    .then_inc(S("h_ready"), 1)

            def top16(rows_, vals, idx):
                for half in (0, 8):
                    for r, v in zip(rows_, vals):
                        did(dve.max(v[:, half:half + 8], r))
                    settle()
                    for r, v, x in zip(rows_, vals, idx):
                        did(dve.max_index(x[:, half:half + 8], v[:, half:half + 8], r))
                    settle()
                    if half == 0:
                        for r, v in zip(rows_, vals):
                            did(dve.match_replace(r, v[:, 0:8], r, NEG))
                        settle()

            for c in range(16):
                wait_taken(dve, ("sc", c))
                top16([SCO[:, t, c, :] for t in range(TT)], [TV[:, t, c, :] for t in range(TT)], [TI[:, t, c, :] for t in range(TT)])
            did(dve.tensor_copy(TIF.rearrange("p t c k -> p (t c k)"), TI.rearrange("p t c k -> p (t c k)")))
            for t in range(TT):
                v = TV[:, t].rearrange("p (h j) k -> p h j k", j=2)
                did(dve.tensor_tensor(CAND[:, t].rearrange("p (h a b) -> p h a b", h=HEADS, a=TOPK),
                                      each(v[:, :, 0, :], TOPK),
                                      v[:, :, 1, :].rearrange("p h (o k) -> p h o k", o=1).broadcast_to([P, HEADS, TOPK, TOPK]),
                                      ALU.add))
            settle()
            for h in range(HEADS):
                top16([CAND[:, t, 256 * h:256 * h + 256] for t in range(TT)], [TS[:, t, h, :] for t in range(TT)],
                      [TP[:, t, h, :] for t in range(TT)])
            tp = TP.rearrange("p t h k -> p (t h k)")
            did(dve.tensor_scalar(TB, tp, 15, None, ALU.bitwise_and))
            settle()
            did(dve.tensor_copy(TBF.rearrange("p t h k -> p (t h k)"), TB))
            settle()
            did(dve.tensor_scalar(TB, tp, 4, None, ALU.logical_shift_right))
            settle()
            did(dve.tensor_copy(TAF.rearrange("p t h k -> p (t h k)"), TB))
            settle()
            iota = cst("iota").rearrange("p (o q k) -> p o q k", o=1, q=1).broadcast_to([P, HEADS, TOPK, TOPK])
            for t in range(TT):
                f = TIF[:, t].rearrange("p (h j) k -> p h j k", j=2)
                for rank, j, dst, hot in ((TAF, 0, EA, HOT), (TBF, 1, EB, HOT2)):
                    hv = hot.rearrange("p (h a b) -> p h a b", h=HEADS, a=TOPK)
                    did(dve.tensor_tensor(hv, each(rank[:, t], TOPK), iota, ALU.is_equal))
                    settle()
                    did(dve.tensor_tensor(hv, hv, f[:, :, j, :].rearrange("p h (o k) -> p h o k", o=1)
                                          .broadcast_to([P, HEADS, TOPK, TOPK]), ALU.mult))
                    settle()
                    did(dve.tensor_reduce(dst[:, t].rearrange("p (h k) -> p h k", h=HEADS), hv, AX.X, ALU.add))
            settle()
            ea, eb = EA.rearrange("p t n -> p (t n)"), EB.rearrange("p t n -> p (t n)")
            did(dve.scalar_tensor_tensor(eb, ea, 128.0, eb, ALU.mult, ALU.add))
            settle()
            dve.tensor_copy(EIDX.rearrange("p t n -> p (t n)"), eb).then_inc(S("experts_ready"), 1)
            ts = TS.rearrange("p t h k -> p (t h) k")
            dve.tensor_tensor(ea.rearrange("p (a k) -> p a k", k=TOPK), ts, ts[:, :, 0:1].broadcast_to([P, 16, TOPK]),
                              ALU.subtract).then_inc(S("top_shifted"), 1)
            dve.wait_ge(S("top_exp"), 1)
            gt = GT.rearrange("p t h k -> p (t h) k")
            did(dve.tensor_reduce(GS_, gt, AX.X, ALU.add))
            settle()
            did(dve.reciprocal(GS_, GS_))
            settle()
            did(dve.tensor_tensor(gt, gt, GS_.rearrange("p (a o) -> p a o", o=1).broadcast_to([P, 16, TOPK]), ALU.mult))
            did(dve.memset(YF.rearrange("p t n -> p (t n)"), 0.0))
            settle()
            for i in range(4):
                wait_taken(dve, ("h2", i))
            gflat = GT.rearrange("p t h k -> p t (h k)")
            for tt in range(TT):
                with dve.Fori(0, NIT) as i:
                    n0 = tt * SPT

                    def add_value(k):
                        b = k % NB
                        dve.wait_ge(S("weight_ready"), n0 + k + 2 + i * BODY)
                        if k:
                            dve.wait_ge(S(f"uv_used{(k - 1) % NB}"), tt * 2 * NIT + (k - 1) // NB + 1 + i * 2)
                        dve.scalar_tensor_tensor(YF[:, tt, :], UV[b][:, D:2 * D], W16[:, k:k + 1], YF[:, tt, :],
                                                 ALU.mult, ALU.add).then_inc(S(f"uv_used{b}"), 1)

                    dve.wait_ge(S("weight_ready"), n0 + 1 + i * BODY)
                    dve.tensor_copy(G16, gflat[:, tt, bass.ds(i * BODY, BODY)]).then_inc(S("slot_gates"), 1)
                    dve.wait_ge(S("slot_gates"), tt * NIT + 1 + i)
                    for k in range(BODY):
                        b, use = k % NB, tt * 2 * NIT + k // NB + 1
                        dve.wait_ge(S(f"uv_landed{b}"), 16 * use + i * 32)
                        if k:
                            dve.wait_ge(S("dot_ready"), n0 + k + i * BODY)
                        dve.tensor_tensor_reduce(PRODS[k % 2], UV[b][:, 0:D], H2T[:, tt, :], 1.0, 0.0, ALU.mult, ALU.add,
                                                 DOT[:, k:k + 1]).then_inc(S("dot_ready"), 1)
                        if k:
                            add_value(k - 1)
                    add_value(BODY - 1)

            dve.wait_ge(S("x_scaled"), 2)
            for i in range(4):
                wait_made(dve, ("yt", i))
                for c in range(2):
                    k = 2 * i + c
                    ins = dve.scalar_tensor_tensor(X[:, k, :], bank(("yt", i))[:, c * TOK:(c + 1) * TOK],
                                                   mod[:, 40 + k:41 + k], X[:, k, :], ALU.mult, ALU.add)
                    if c:
                        taken(ins, ("yt", i))
                    else:
                        did(ins)
            settle()
            layer_norm(2, "ln2_g", "ln2_b")
            for c in range(DC):
                dve.tensor_scalar(X[:, c, :], X[:, c, :], pc("ln2_b", c), None, ALU.add).then_inc(S("x_ready"), 1)
            dve.wait_ge(S("x_ready"), DC)

            def rms_norm(job, i, g, g0, out_sem="h_ready"):
                wait_made(dve, job)
                taken(dve.tensor_scalar(RS[:, :], bank(job)[:, 0:TOK], 1.0 / D, EPS_2, ALU.mult, ALU.add), job)
                wait_taken(dve, job)
                dve.reciprocal(RS[:, :], RS[:, :]).then_inc(S("rms_inv"), 1)
                dve.wait_ge(S("rms_rstd"), i)
                for c in range(DC):
                    dve.scalar_tensor_tensor(H[:, c, :], X[:, c, :], pc(g, g0 + c), RS[:, :], ALU.mult, ALU.mult)\
                        .then_inc(S(out_sem), 1)

            dve.scalar_tensor_tensor(RGC[:, 0:8], pc("rec_lambda", 0, 8), -1.0, pc("rec_lambda", 0, 8), ALU.mult, ALU.min).then_inc(S("lam_negabs"), 1)
            did(dve.tensor_scalar(small[:, 232:240], pc("rec_lambda", 0, 8), 0.0, None, ALU.min))
            dve.wait_ge(S("lam_ln"), 1)
            settle()
            did(dve.scalar_tensor_tensor(RGC[:, 0:8], RGC[:, 0:8], -1.0, small[:, 232:240], ALU.mult, ALU.add))
            settle()
            did(dve.tensor_scalar(RGC[:, 0:8], RGC[:, 0:8], RG_C, None, ALU.mult))
            rms_norm("rms_mix0", 1, "mix_g", 0)
            for t in range(4, 8):
                wait_evacuated(dve, "rec_in", t)
            conv(0, 8, XR, "rec_conv_w", "rec_conv_b", 8, XCV, "xcv_sum")
            for c in range(DC):
                wait_taken(dve, ("rg", c))
                dve.tensor_scalar(RR[:, c, :], RR[:, c, :], RGC[:, c:c + 1], None, ALU.mult).then_inc(S("log_a"), 1)
            did(dve.tensor_tensor(XCV[:, :, :], XCV[:, :, :], II[:, :, :], ALU.mult))
            dve.wait_ge(S("a_ready"), 1)
            did(dve.tensor_tensor(T1[:, :, :], AA[:, :, :], AA[:, :, :], ALU.mult))
            settle()
            dve.scalar_tensor_tensor(T1[:, :, :], T1[:, :, :], 1.0, RR[:, :, :], ALU.add, ALU.mult).then_inc(S("u_square"), 1)
            dve.wait_ge(S("u_root"), 1)
            did(dve.tensor_tensor(T1[:, :, :], T1[:, :, :], XCV[:, :, :], ALU.mult))
            settle()
            for c in range(DC):
                did(dve.tensor_tensor_scan(YR[:, c, :], AA[:, c, :], T1[:, c, :], 0.0, ALU.mult, ALU.add))
            settle()
            for t in range(4):
                wait_evacuated(dve, "rec_in", t)
            dve.tensor_tensor(YR[:, :, :], YR[:, :, :], GATE[:, :, :], ALU.mult).then_inc(S("yr_ready"), 1)

            def residual(name):
                for t in range(4):
                    n = colt(name, t)
                    wait_column(dve, name, t)
                    for c in range(2):
                        k = 2 * t + c
                        evacuated(dve.tensor_tensor(X[:, k, :], acc(n, c), X[:, k, :], ALU.add), name, t)
                wait_evacuated(dve, name, 2)
                wait_evacuated(dve, name, 3)

            def mlp(layer):
                up, down = f"up{layer}", f"down{layer}"
                n0 = COLT0[up]
                with dve.Fori(0, 4) as i:
                    for s in range(4):
                        n = n0 + s
                        for c in range(2):
                            dve.wait_ge(S(f"pair_taken{n % 2}"), 2 * (n // 2) + c + 1 + i * 4)
                            r = RL[2 * s + c]
                            dve.tensor_tensor(HID[:, bass.ds(8 * i + (2 * s + c), 1), :].rearrange("p o n -> p (o n)"), r, r,
                                              ALU.mult).then_inc(S("hidden"), 1)
                n0, t0 = COLT0[down], TILE0[down]
                with dve.Fori(0, 2) as i:
                    for half in range(2):
                        n = n0 + half
                        s = t0 + 4 * half + 3
                        dve.wait_ge(S(f"tile_used{s % SLOTS}"), s // SLOTS + 1 + i * 2)
                        for c in range(2):
                            x = X[:, bass.ds(4 * i + (2 * half + c), 1), :].rearrange("p o n -> p (o n)")
                            dve.tensor_tensor(x, acc(n, c), x, ALU.add).then_inc(S(f"pair_taken{n % 2}"), 1)
                wait_evacuated(dve, down, 2)
                wait_evacuated(dve, down, 3)

            residual("rec_out")
            dve.memset(small[:, 224:225], 0.0).then_inc(S("hidden"), 1)
            rms_norm("rms_mlp0", 2, "mlp_g", 0)
            mlp(0)
            rms_norm("rms_mix1", 3, "mix_g", 8)
            wait_made(dve, "wi")
            taken(dve.tensor_scalar(WI[:, :, :], bank("wi")[:, 0:16].rearrange("p (t h) -> p t h", t=TT), IDX_W_SCALE, None,
                                    ALU.mult), "wi")
            wait_made(dve, "rms_c")
            taken(dve.tensor_scalar(RS[:, :], bank("rms_c")[:, 0:TOK], 1.0 / P, EPS_2, ALU.mult, ALU.add), "rms_c")
            wait_taken(dve, "rms_c")
            dve.reciprocal(RS[:, :], RS[:, :]).then_inc(S("c_inv"), 1)
            dve.wait_ge(S("c_rstd"), 1)
            dve.scalar_tensor_tensor(CN, CR, pc("kv_g"), RS[:, :], ALU.mult, ALU.mult).then_inc(S("cn_ready"), 1)

            halves = ((0, P), (P, WIDE))
            for h in range(H_IDX):
                wait_made(dve, ("dot", h))
                b = bank(("dot", h))
                dst = SCW if h == 0 else (TMP, TMP2)[h % 2]
                did(dve.tensor_scalar(dst[:, 0:P], b[:, 0:P], 0.0, WI[:, 0, h:h + 1], ALU.max, ALU.mult))
                taken(dve.tensor_scalar(dst[:, P:WIDE], b[:, P:WIDE], 0.0, WI[:, 1, h:h + 1], ALU.max, ALU.mult), ("dot", h))
                wait_taken(dve, ("dot", h))
                settle()
                if h:
                    did(dve.tensor_tensor(SCW, SCW, dst, ALU.add))
                    settle()
            did(dve.tensor_scalar(MSK, cst("dist"), 0.5 * FAR, None, ALU.is_lt))
            settle()
            did(dve.tensor_scalar(TMP, MSK, -1.0, FAR, ALU.add, ALU.mult))
            did(dve.tensor_tensor(SCW, SCW, MSK, ALU.mult))
            settle()
            did(dve.tensor_tensor(SCW, SCW, TMP, ALU.add))
            settle()
            for r in range(KEEP // 8):
                for x, y in halves:
                    did(dve.max(MX[:, 8 * (x > 0):8 * (x > 0) + 8], SCW[:, x:y]))
                settle()
                for x, y in halves:
                    did(dve.match_replace(SCW[:, x:y], MX[:, 8 * (x > 0):8 * (x > 0) + 8], SCW[:, x:y], NEG))
                settle()
            did(dve.tensor_scalar(SCW, SCW, NEG, None, ALU.is_equal))
            settle()
            did(dve.tensor_tensor(MSK, MSK, SCW, ALU.mult))
            settle()
            did(dve.tensor_scalar(MSK, MSK, -1.0, FAR, ALU.add, ALU.mult))
            settle()
            def logit(h):
                wait_made(dve, ("lg", h))
                p = PR[h % 4]
                if h >= 4:
                    wait_made(dve, ("pt", h - 4))
                b = bank(("lg", h))
                m = MX[:, 2 * (h % 4):2 * (h % 4) + 2]
                did(dve.tensor_tensor_reduce(p[:, 0:P], b[:, 0:P], MSK[:, 0:P], 1.0, NEG, ALU.add, ALU.max, m[:, 0:1]))
                taken(dve.tensor_tensor_reduce(p[:, P:WIDE], b[:, P:WIDE], MSK[:, P:WIDE], 1.0, NEG, ALU.add, ALU.max,
                                               m[:, 1:2]), ("lg", h))
                wait_taken(dve, ("lg", h))
                dve.tensor_scalar(m, m, -1.0, None, ALU.mult).then_inc(S("lg_negmax"), 1)

            logit(0)
            for h in range(H_ATT):
                if h + 1 < H_ATT:
                    logit(h + 1)
                dve.wait_ge(S("lg_exp"), 2 * (h + 1))
                sm = SM[:, 2 * (h % 4):2 * (h % 4) + 2]
                did(dve.reciprocal(sm, sm))
                settle()
                p = PR[h % 4]
                did(dve.tensor_scalar(p[:, 0:P], p[:, 0:P], sm[:, 0:1], None, ALU.mult))
                settle()
                dve.tensor_scalar(p[:, P:WIDE], p[:, P:WIDE], sm[:, 1:2], None, ALU.mult).then_inc(S("p_ready"), 1)
            residual("att_out")
            rms_norm("rms_mlp1", 4, "mlp_g", 8)
            mlp(1)
            rms_norm("rms_fin", 5, "final_g", 0, "out_ready")


def lay_out(np_, inputs):
    a = {k: np_.asarray(v) for k, v in inputs.items()}

    def tiles(w):
        i, o = w.shape
        return w.reshape(i // D, DC, P, o // COLS, COLS).transpose(3, 0, 2, 1, 4).reshape(-1, P, TILE)

    def cols(v):
        return v.reshape(-1, P).T

    w_in = a["w_in"][0]
    q, k, v, z, xbc, dt, g = np_.split(w_in, [1024, 2048, 3072, 5120, 8192, 8224], axis=1)
    att = a["att_w_in_2"][0]
    ki = att[:, 1664:1728]
    att_cols = np_.concatenate([att[:, 0:1664], ki, ki], axis=1)
    uk = a["att_w_uk_2"][0].reshape(8, P, P).transpose(1, 0, 2).reshape(P, 1024)
    uv = a["att_w_uv_2"][0].transpose(1, 0, 2).reshape(P, 1024)
    parts = [q, k, v, xbc, z, g, a["w_attn_branch"][0], a["w_ssd_branch"][0], a["w_out"][0], a["peer_w_query"][0],
             a["rec_w_in_2"][0], a["rec_w_out_2"][0], a["mlp_w_up_2"][0], a["mlp_w_down_2"][0], att_cols, None,
             a["att_w_o_2"][0], a["mlp_w_up_2"][1], a["mlp_w_down_2"][1]]
    stream = np_.concatenate([tiles(w) if w is not None else np_.concatenate([uk, uv], axis=1)[None] for w in parts])
    f = np_.float32
    p_, m_ = np_.arange(P), np_.arange(TOK)

    def dist(q0, n):
        d = (q0 + p_[:, None] - np_.arange(n)[None, :]).astype(f)
        return np_.where(d >= 0, d, f(FAR)).astype(f)

    con = np_.concatenate([np_.eye(P, dtype=f), np_.ones((P, P), f), dist(0, P), dist(P, TOK),
                           (p_[:, None] <= m_[None, :]).astype(f), np_.tile(np_.arange(TOPK, dtype=f), (P, 1)),
                           np_.eye(P, dtype=f)[::-1]], axis=1)
    n = np_.maximum(TOK - 1 - np_.arange(WIDE), 0)
    large = 16 + (np_.log(np_.maximum(n, 1).astype(f) / f(16)) / f(math.log(8.0)) * f(16)).astype(np_.int32)
    bucket = np_.where(n < 16, n, np_.minimum(large, BUCKETS - 1))
    rg = np_.stack([a["rec_w_a_2"][0], a["rec_w_x_2"][0]]).reshape(2, 8, P, 256).transpose(2, 0, 1, 3).reshape(P, 4096)
    par = [a["b_ada"], a["conv_w"][0], a["conv_b"], a["ssd_norm_w"], np_.repeat(a["d_skip"][0], 64), a["da_subln_w"],
           a["ln1_g"], a["ln1_b"], a["ln2_g"], a["ln2_b"], a["norm_mix_g_2"], a["norm_mlp_g_2"], a["final_norm_g_2"],
           a["rec_conv_w_2"][0], a["rec_conv_b_2"], a["rec_b_a_2"], a["rec_b_x_2"], a["rec_lambda_2"],
           a["att_kv_norm_g_2"], a["c"]]
    rows = np_.concatenate([a[x][0] for x, _ in ROWS])
    return {
        "stream": stream,
        "ada": tiles(a["w_ada"][0]),
        "par": np_.concatenate([cols(x) for x in par], axis=1),
        "rows": np_.tile(rows, (P, 1)),
        "con": con,
        "xT": a["x"][0].T.reshape(DC, P, TOK).transpose(1, 0, 2),
        "wdt": dt.reshape(DC, P, 32).transpose(1, 0, 2),
        "sk": a["peer_sub_keys"][0].transpose(2, 0, 1).reshape(P, 2 * P),
        "peer_uv": np_.concatenate([a["peer_u"][0], a["peer_v"][0]], axis=1),
        "rgw": rg,
        "wwi": att[:, 1728:1736].reshape(DC, P, 8).transpose(1, 0, 2),
        "selh": (np_.arange(BUCKETS)[:, None] == bucket[None, :]).astype(f),
        "relb": a["rel_bias_2"],
    }


def kernel(**inputs):
    import numpy as _np
    import concourse.bacc as _bacc
    from concourse import mybir as _mybir
    from concourse.bass_utils import run_bass_kernel_spmd as _run

    nc = _bacc.Bacc("TRN2", target_bir_lowering=False, num_devices=1)
    arrays, io = {}, {}
    for name, a in lay_out(_np, inputs).items():
        a = _np.ascontiguousarray(a)
        arrays[f"in_{name}_dram"] = a
        io[name] = nc.dram_tensor(f"in_{name}_dram", a.shape, _mybir.dt.from_np(a.dtype), kind="ExternalInput").ap()
    io["bv"] = nc.dram_tensor("bias_by_distance", (H_ATT, WIDE), F32, kind="Internal").ap()
    io["outT"] = nc.dram_tensor("out_0_dram", (P, DC, TOK), F32, kind="ExternalOutput").ap()
    program(nc, io)
    r = _run(nc, [arrays], core_ids=[0])
    out = r.results[0]["out_0_dram"]
    return out.transpose(2, 1, 0).reshape(1, TOK, D)
```

```python
import math
from contextlib import ExitStack

import concourse.bass as bass
import numpy as np
from concourse import mybir

F32 = mybir.dt.float32
U32 = mybir.dt.uint32
ALU = mybir.AluOpType
ACT = mybir.ActivationFunctionType
AX = mybir.AxisListType

P = 128
TOK = 256
TT = TOK // P
D = 1024
DC = D // P
COLS = 256
SLOTS = 4
TILE = DC * COLS
NEG = -3.0e38
FAR = 1.0e30

HEADS = 8
DA_SCALE = 64 ** -0.5
LAMBDA_INIT = 0.8 - 0.6 * math.exp(0.0)
SSD_HEADS = 32
GROUPS = 4
EPS = 1e-5
EPS_2 = 1e-6
ALPHA = 2.0 ** 0.25
TOPK = 16
EXPERTS = 128 * 128
RG_C = 8.0
H_ATT = 16
H_IDX = 8
ATT_SCALE = 64 ** -0.5
IDX_W_SCALE = (8 ** -0.5) * (64 ** -0.5)
KEEP = 64
BUCKETS = 32
WIDE = P + TOK

STREAM = [("q", 1, 4), ("k", 1, 4), ("v", 1, 4), ("xbc", 1, 12), ("z", 1, 8), ("g", 1, 8),
          ("attn", 1, 4), ("ssd", 2, 4), ("out", 1, 4), ("query", 1, 8),
          ("rec_in", 1, 8), ("rec_out", 1, 4), ("up0", 1, 16), ("down0", 4, 4),
          ("att_in", 1, 7), ("uk_uv", 1, 1), ("att_out", 1, 4), ("up1", 1, 16), ("down1", 4, 4)]
TILE0, COLT0 = {}, {}


def _number_tiles():
    tile, colt = 0, 0
    for name, groups, cols in STREAM:
        TILE0[name], COLT0[name] = tile, colt
        tile += groups * cols
        colt += 0 if name == "uk_uv" else cols
    return tile


N_TILES = _number_tiles()

PARAMS = [("b_ada", 48), ("conv_w", 96), ("conv_b", 24), ("ssd_norm_w", 16), ("d_skip", 16), ("subln", 1),
          ("ln1_g", 8), ("ln1_b", 8), ("ln2_g", 8), ("ln2_b", 8), ("mix_g", 16), ("mlp_g", 16), ("final_g", 8),
          ("rec_conv_w", 32), ("rec_conv_b", 8), ("rec_b_a", 8), ("rec_b_x", 8), ("rec_lambda", 8),
          ("kv_g", 1), ("c", 8)]
ROWS = [("dt_bias", 32), ("a_log", 32), ("lambda_q1", 64), ("lambda_k1", 64), ("lambda_q2", 64), ("lambda_k2", 64)]
CONSTS = [("ident", P), ("ones", P), ("dist", WIDE), ("triu", TOK), ("iota", TOPK), ("flip", P)]


def offsets(table):
    at, out = 0, {}
    for name, n in table:
        out[name] = (at, at + n)
        at += n
    return out, at


def plan_jobs():
    jobs = ["mod_a"]
    jobs += [("s", 0, 0), ("s", 0, 1)]
    for h in range(HEADS):
        if h == 1:
            jobs.append("dt")
        if h == 4:
            jobs += ["mod_b", "cum0", "cum1"]
        jobs.append(("t", h))
        if h + 1 < HEADS:
            jobs += [("s", h + 1, 0), ("s", h + 1, 1)]
        jobs.append(("o", h))
    jobs += [("yn", h) for h in range(HEADS)]
    jobs += [("xs", i) for i in range(8)] + [("cb", g) for g in range(GROUPS)]
    jobs += [("cr", 0), ("cr", 1)]
    for pair in range(SSD_HEADS // 2):
        if pair + 1 < SSD_HEADS // 2:
            jobs += [("cr", 2 * pair + 2), ("cr", 2 * pair + 3)]
        jobs.append(("y", pair))
    jobs += [("gn", g) for g in range(GROUPS)]
    jobs += ["mean1", "var1"]
    jobs += [("h2", i) for i in range(4)]
    jobs += [("sc", c) for c in range(16)]
    jobs += [("yt", i) for i in range(4)] + ["mean2", "var2"]
    jobs += ["rms_mix0"] + [("rg", c) for c in range(8)] + ["rms_mlp0"]
    jobs += ["bv", "rms_mix1", "wi", "rms_c", "ctok"] + [("dot", h) for h in range(H_IDX)]
    jobs += [("ql", h) for h in range(H_ATT)]
    jobs += [("lg", 0), ("lg", 1)]
    for h in range(H_ATT):
        if h + 2 < H_ATT:
            jobs.append(("lg", h + 2))
        jobs += [("pt", h), ("ol", h)]
        if h % 2 == 1:
            jobs.append(("ot", h // 2))
    jobs += ["rms_mlp1", "rms_fin"]
    return {name: n for n, name in enumerate(jobs)}


JOBS = plan_jobs()


def beside_head(h):
    return [("xbc", t) for t in range(3 * h, 3 * h + 3)] if h < 4 else [("z", t) for t in range(2 * h - 8, 2 * h - 6)]


def program(nc, io):
    PO, NPAR = offsets(PARAMS)
    RO, NROW = offsets(ROWS)
    CO, NCON = offsets(CONSTS)
    ctx = ExitStack()
    with ctx:
        def sb(name, shape, dt=F32):
            return ctx.enter_context(nc.sbuf_tensor(name, shape, dt))

        sems = {}

        def S(name):
            if name not in sems:
                sems[name] = ctx.enter_context(nc.semaphore(name))
            return sems[name]

        ring = sb("ring", [P, SLOTS, TILE])
        X = sb("X", [P, DC, TOK])
        H = sb("H", [P, DC, TOK])
        PROJ = sb("PROJ", [P, 72, TOK])
        V = sb("V", [P, TT, D])
        CONV = sb("CONV", [P, 24, TOK])
        AUX = sb("AUX", [P, 32, TOK])
        SCR = sb("SCR", [P, 3840])
        par = sb("par", [P, NPAR])
        con = sb("con", [P, NCON])
        mod = sb("mod", [P, 48])
        dts = sb("dts", [P, 7, TT, 32])
        small = sb("small", [P, 256])
        wdt = PROJ[:, 71, :].rearrange("p (k n) -> p k n", k=DC)
        rows = PROJ[:, 69:71, :].rearrange("p a b -> p (a b)")[:, 0:NROW]
        RS = AUX[:, 31, :]
        PS = ctx.enter_context(nc.psum_tensor("PS", [P, 8, 512], F32))

        def pc(name, i=0, n=1):
            a = PO[name][0] + i
            return par[:, a:a + n]

        def row(name):
            return rows[:, RO[name][0]:RO[name][1]]

        def cst(name, a=0, b=None):
            return con[:, CO[name][0] + a:CO[name][1] if b is None else CO[name][0] + b]

        ident, ones = cst("ident"), cst("ones")

        def flat(ap):
            return ap.rearrange("p a b -> p (a b)")

        def over(ap, n):
            return ap.rearrange("p (o k) -> p o k", o=1).broadcast_to([P, n, ap.shape[1]])

        def each(ap, n):
            return ap.rearrange("p a (b o) -> p a b o", o=1).broadcast_to([P, ap.shape[1], ap.shape[2], n])

        Q, K, Z, XBC, G = (PROJ[:, a:b, :] for a, b in ((0, 8), (8, 16), (16, 32), (32, 56), (56, 72)))
        YA, MIX, YS = PROJ[:, 0:8, :], PROJ[:, 8:16, :], PROJ[:, 32:48, :]
        SC = [[SCR[:, (2 * b + j) * WIDE:(2 * b + j + 1) * WIDE] for j in range(2)] for b in range(2)]
        AM = [SCR[:, (4 + b) * WIDE:(5 + b) * WIDE] for b in range(2)]
        AT = [SCR[:, (6 + b) * WIDE:(7 + b) * WIDE] for b in range(2)]
        AB = [SCR[:, (8 + b) * WIDE:(9 + b) * WIDE] for b in range(2)]
        adaW = AUX[:, :, :].rearrange("p (s k) n -> p s k n", s=SLOTS)
        adaE = PROJ[:, 8:40, :].rearrange("p (s k) n -> p s k n", s=SLOTS)

        def ada_done(i, s):
            return 4 * DC * i + 2 * DC * (s // 2) + 2 * (DC - 1) + s % 2 + 1

        XDT = flat(AUX[:, 0:16, :]).rearrange("p (t n) -> p t n", t=TT)
        CB = flat(AUX[:, 16:22, :]).rearrange("p (g n) -> p g n", g=GROUPS)
        SEG = flat(AUX[:, 22:28, :]).rearrange("p (b n) -> p b n", n=WIDE)
        dt_, dtA, cum, dtx, dty, dtz, arow = (dts[:, i] for i in range(7))

        def bank(job):
            return PS[:, 4 + JOBS[job] % 4, :]

        def wait_made(e, job):
            n = JOBS[job]
            e.wait_ge(S(f"job_made{n % 4}"), n // 4 + 1)

        def made(ins, job):
            ins.then_inc(S(f"job_made{JOBS[job] % 4}"), 1)

        def wait_taken(e, job):
            n = JOBS[job]
            e.wait_ge(S(f"job_taken{n % 4}"), n // 4 + 1)

        def taken(ins, job):
            ins.then_inc(S(f"job_taken{JOBS[job] % 4}"), 1)

        def open_bank(e, job):
            n = JOBS[job]
            if n >= 4:
                e.wait_ge(S(f"job_taken{n % 4}"), n // 4)
            return PS[:, 4 + n % 4, :]

        def colt(name, t):
            return COLT0[name] + t

        def acc(n, c):
            return PS[:, 2 * (n % 2) + c, 0:TOK]

        def wait_column(e, name, t, groups=1):
            last = TILE0[name] + t * groups + groups - 1
            e.wait_ge(S(f"tile_used{last % SLOTS}"), last // SLOTS + 1)

        def evacuated(ins, name, t):
            ins.then_inc(S(f"pair_taken{colt(name, t) % 2}"), 1)

        def wait_evacuated(e, name, t):
            n = colt(name, t)
            e.wait_ge(S(f"pair_taken{n % 2}"), 2 * (n // 2 + 1))

        for s in range(SLOTS):
            S(f"tile_landed{s}"), S(f"tile_used{s}"), S(f"job_made{s}"), S(f"job_taken{s}")
        S("pair_taken0"), S("pair_taken1")

        class Steps:

            def __init__(self, eng, name):
                self.eng, self.sem, self.n = eng, S(name), 0

            def did(self, ins):
                ins.then_inc(self.sem, 1)
                self.n += 1

            def settle(self):
                self.eng.wait_ge(self.sem, self.n)

        UV = [flat(AUX[:, 8 * i:8 * i + 8, :]) for i in range(4)] + \
             [flat(CONV[:, 8 * i:8 * i + 8, :]) for i in range(3)] + [flat(V[:, :, :])]
        NB = len(UV)
        BODY = 2 * NB
        SPT = HEADS * TOPK
        NIT = SPT // BODY
        H2T = flat(PROJ[:, 0:8, :]).rearrange("p (t n) -> p t n", t=TT)
        YF = flat(PROJ[:, 8:16, :]).rearrange("p (t n) -> p t n", t=TT)
        QT = PROJ[:, 16:32, :]
        SCO = flat(PROJ[:, 32:48, :]).rearrange("p (t c n) -> p t c n", t=TT, c=16)
        CAND = flat(PROJ[:, 48:64, :]).rearrange("p (t n) -> p t n", t=TT)
        HOT = flat(PROJ[:, 64:66, :]).rearrange("p (j a b) -> p j a b", j=2, a=TOPK)
        TV = SCR[:, 0:512].rearrange("p (t c k) -> p t c k", t=TT, c=16)
        TI = SCR[:, 512:1024].bitcast(U32).rearrange("p (t c k) -> p t c k", t=TT, c=16)
        TIF = SCR[:, 1024:1536].rearrange("p (t c k) -> p t c k", t=TT, c=16)
        TS = SCR[:, 1536:1792].rearrange("p (t h k) -> p t h k", t=TT, h=HEADS)
        TP = SCR[:, 1792:2048].bitcast(U32).rearrange("p (t h k) -> p t h k", t=TT, h=HEADS)
        RANK = SCR[:, 2048:2080].bitcast(U32).rearrange("p (j k) -> p j k", j=2)
        RANKF = SCR[:, 2304:2336].rearrange("p (j k) -> p j k", j=2)
        KEYS = SCR[:, 2816:2848].rearrange("p (j k) -> p j k", j=2)
        EIDX = SCR[:, 3328:3584].bitcast(U32).rearrange("p (t n) -> p t n", t=TT)
        GT = SCR[:, 3584:3840].rearrange("p (t h k) -> p t h k", t=TT, h=HEADS)
        GS_ = small[:, 128:136]
        EPS_COL, EPS2_COL = small[:, 225:226], small[:, 226:227]
        H_GAIN, H_SHIFT, X_GAIN, X_SHIFT = (small[:, a:a + 8] for a in (96, 104, 112, 120))
        G16 = small[:, 160:176]
        DOT = small[:, 176:192]
        GEL = small[:, 192:208]
        W16 = small[:, 208:224]
        PRODS = [flat(PROJ[:, 48 + 4 * i:52 + 4 * i, :]) for i in range(2)]

        GATE, XR, XCV, RR, II, AA, T1, YR = (PROJ[:, 8 * i:8 * i + 8, :] for i in range(8))
        RGW = flat(CONV[:, 0:16, :]).rearrange("p (g n i m) -> p g n i m", g=2, n=8, i=2)
        HID = PROJ[:, 0:32, :]
        RL = [PROJ[:, 32 + i, :] for i in range(8)]
        SQ2 = PROJ[:, 64:72, :]
        BIAS = flat(CONV[:, :, :]).rearrange("p (h n) -> p h n", h=H_ATT)
        QT2, QI, KI, CR, CN = PROJ[:, 0:8, :], PROJ[:, 8:12, :], PROJ[:, 12, :], PROJ[:, 13, :], PROJ[:, 14, :]
        CTOK = PROJ[:, 15, :].rearrange("p (t c) -> p t c", t=TT)
        QLAT = PROJ[:, 16:32, :]
        w8 = flat(PROJ[:, 32:56, :]).rearrange("p (n k) -> p n k", k=WIDE)
        SCW, TMP, TMP2, MSK = w8[:, 0, :], w8[:, 1, :], w8[:, 2, :], w8[:, 3, :]
        PR = [w8[:, 4 + i, :] for i in range(4)]
        PT = [w8[:, 8 + i, :] for i in range(2)]
        OL = [w8[:, 10 + i, 0:TOK] for i in range(4)]
        OT = PROJ[:, 56:64, :]
        WI = small[:, 0:16].rearrange("p (t h) -> p t h", t=TT)
        BVS = AUX[0:16, 0:2, :].rearrange("p a b -> p (a b)")
        WWI = flat(AUX[:, 2:4, :])[:, 0:64].rearrange("p (k h) -> p k h", k=DC)
        SELH = flat(AUX[:, 4:6, :])[0:BUCKETS, 0:WIDE]
        RELB = flat(AUX[:, 6:8, :])[0:BUCKETS, 0:H_ATT]
        SK = PROJ[:, 70, :].rearrange("p (j k) -> p j k", j=2)
        RGC = small[:, 16:32]
        MX, SM = small[:, 32:64], small[:, 64:96]

        def SQA(h):
            return PROJ[:, 8 + h, :]

        ukuv = ring[:, (TILE0["uk_uv"]) % SLOTS, :]
        UK = ukuv[:, 0:1024].rearrange("p (g c) -> p g c", g=8)
        UVV = ukuv[:, 1024:2048].rearrange("p (h v) -> p h v", h=H_ATT)

        block = ctx.enter_context(nc.Block())

        @block.sync
        def _(sp):
            def load(i, s):
                sp.dma_start(ring[:, s, :], io["stream"][SLOTS * i + s]).then_inc(S(f"tile_landed{s}"), 16)

            sp.dma_start(par[:, :], io["par"]).then_inc(S("params_landed"), 16)
            sp.dma_start(con[:, :], io["con"]).then_inc(S("params_landed"), 16)
            sp.dma_start(X[:, :, :], io["xT"]).then_inc(S("x_landed"), 16)
            sp.wait_ge(S("ada_early3"), 16)
            for s in range(SLOTS):
                load(0, s)
            with sp.Fori(1, N_TILES // SLOTS) as i:
                for s in range(SLOTS):
                    sp.wait_ge(S(f"tile_used{s}"), i)
                    sp.dma_start(ring[:, s, :], io["stream"][bass.ds(SLOTS * i + s, 1)]
                                 .rearrange("o p n -> p (o n)")).then_inc(S(f"tile_landed{s}"), 16)
            sp.wait_ge(S("out_ready"), DC)
            sp.dma_start(io["outT"], H[:, :, :]).then_inc(S("out_stored"), 16)
            sp.wait_ge(S("out_stored"), 16)

        @block.tensor
        def _(pe):
            def tile_wait(name, i):
                t = TILE0[name] + i
                pe.wait_ge(S(f"tile_landed{t % SLOTS}"), 16 * (t // SLOTS + 1))
                return ring[:, t % SLOTS, :].rearrange("p (k n) -> p k n", k=DC)

            def tile_done(ins, name, i):
                ins.then_inc(S(f"tile_used{(TILE0[name] + i) % SLOTS}"), 1)

            def project(name, t, src, groups=1, ready=None):
                n = colt(name, t)
                if n >= 2:
                    pe.wait_ge(S(f"pair_taken{n % 2}"), 2 * (n // 2))
                for g in range(groups):
                    w = tile_wait(name, t * groups + g)
                    for c in range(2):
                        for k in range(DC):
                            if ready and c == 0:
                                ready(g * DC + k)
                            mm = pe.matmul(acc(n, c), w[:, k, c * P:(c + 1) * P], src[:, g * DC + k, :],
                                           start=(g == 0 and k == 0), stop=(g == groups - 1 and k == DC - 1))
                    tile_done(mm, name, t * groups + g)

            def h_from(i):
                return lambda k: pe.wait_ge(S("h_ready"), i * DC + k + 1)

            def taken_from(name):
                def ready(k):
                    n = colt(name, k // 2)
                    pe.wait_ge(S(f"pair_taken{n % 2}"), 2 * (n // 2) + k % 2 + 1)
                return ready

            def sum_chunks(job, src, n, width=TOK, ready=None):
                o = open_bank(pe, job)
                for k in range(n):
                    if ready:
                        ready(k)
                    mm = pe.matmul(o[:, 0:width], ones, src[:, k, :], start=(k == 0), stop=(k == n - 1))
                made(mm, job)

            pe.wait_ge(S("params_landed"), 32)

            o = open_bank(pe, "mod_a")
            for i in range(8):
                pe.wait_ge(S("ada_tiles"), ada_done(i // SLOTS, i % SLOTS))
                for c in range(2):
                    mm = pe.matmul(o[:, 2 * i + c:2 * i + c + 1], CONV[:, 16 + i, c * P:(c + 1) * P], ones[:, 0:1],
                                   start=(i + c == 0), stop=True, skip_group_check=True)
            made(mm, "mod_a")

            for t in range(4):
                project("q", t, H, ready=None if t else h_from(0))
            for t in range(4):
                project("k", t, H)
            for t in range(4):
                n = colt("v", t)
                pe.wait_ge(S(f"pair_taken{n % 2}"), 2 * (n // 2))
                w = tile_wait("v", t)
                for c in range(TT):
                    for k in range(DC):
                        mm = pe.matmul(acc(n, c), H[:, k, c * P:(c + 1) * P], w[:, k, :], start=(k == 0), stop=(k == DC - 1))
                tile_done(mm, "v", t)

            def scores(h):
                for j in range(2):
                    o = open_bank(pe, ("s", h, j))
                    q, k = Q[64 * j:64 * j + 64, h, :], K[64 * j:64 * j + 64, h, :]
                    pe.matmul(o[:, 0:P], q[:, 0:P], k[:, 0:P], start=True, stop=True)
                    mm = pe.matmul(o[:, P:WIDE], q[:, P:TOK], k[:, :], start=True, stop=True)
                    made(mm, ("s", h, j))

            def attend_transpose(h):
                o = open_bank(pe, ("t", h))
                pe.wait_ge(S("da_diff"), h + 1)
                a = AM[h % 2]
                pe.transpose(o[:, 0:P], a[:, 0:P], ident)
                pe.transpose(o[:, P:2 * P], a[:, P:2 * P], ident)
                made(pe.transpose(o[:, 2 * P:3 * P], a[:, 2 * P:3 * P], ident), ("t", h))

            def attend(h):
                o = open_bank(pe, ("o", h))
                wait_taken(pe, ("t", h))
                at = AT[h % 2]
                pe.matmul(o[:, 0:TOK], V[:, 0, h * P:(h + 1) * P], at[:, 0:TOK], start=True, stop=False)
                made(pe.matmul(o[:, P:TOK], V[:, 1, h * P:(h + 1) * P], at[:, TOK:WIDE], start=False, stop=True), ("o", h))

            wait_evacuated(pe, "k", 3)
            wait_evacuated(pe, "k", 2)
            scores(0)
            for h in range(HEADS):
                if h == 1:
                    o = open_bank(pe, "dt")
                    pe.wait_ge(S("wdt_landed"), 16)
                    for t in range(TT):
                        for k in range(DC):
                            mm = pe.matmul(o[:, 32 * t:32 * t + 32], H[:, k, t * P:(t + 1) * P], wdt[:, k, :],
                                           start=(k == 0), stop=(k == DC - 1))
                    made(mm, "dt")
                if h == 4:
                    o = open_bank(pe, "mod_b")
                    pe.wait_ge(S("ada_tiles"), 24 * DC)
                    for i in range(16):
                        for c in range(2):
                            mm = pe.matmul(o[:, 2 * i + c:2 * i + c + 1], CONV[:, i, c * P:(c + 1) * P], ones[:, 0:1],
                                           start=(i + c == 0), stop=True, skip_group_check=True)
                    made(mm, "mod_b")
                    pe.wait_ge(S("dta_ready"), 1)
                    o = open_bank(pe, "cum0")
                    made(pe.matmul(o[:, 0:32], cst("triu", 0, P), dtA[:, 0, :], start=True, stop=True), "cum0")
                    o = open_bank(pe, "cum1")
                    pe.matmul(o[:, 0:32], ones, dtA[:, 0, :], start=True, stop=False)
                    made(pe.matmul(o[:, 0:32], cst("triu", 0, P), dtA[:, 1, :], start=False, stop=True), "cum1")
                for name, t in beside_head(h):
                    project(name, t, H)
                attend_transpose(h)
                if h + 1 < HEADS:
                    scores(h + 1)
                if h == 0:
                    wait_evacuated(pe, "v", 2)
                    wait_evacuated(pe, "v", 3)
                attend(h)
            project("g", 0, H)
            for h in range(HEADS):
                o = open_bank(pe, ("yn", h))
                pe.wait_ge(S("da_square"), h + 1)
                made(pe.matmul(o[:, 0:TOK], ones, SQA(h), start=True, stop=True), ("yn", h))

            project("g", 1, H)
            pe.wait_ge(S("conv_ready"), 24)
            for i in range(8):
                o = open_bank(pe, ("xs", i))
                t, q = i % 2, i // 2
                for c in range(4):
                    mm = pe.transpose(o[:, c * P:(c + 1) * P], CONV[:, 4 * q + c, t * P:(t + 1) * P], ident)
                made(mm, ("xs", i))
            for g in range(GROUPS):
                o = open_bank(pe, ("cb", g))
                b, c = CONV[:, 16 + g, :], CONV[:, 20 + g, :]
                pe.matmul(o[:, 0:TOK], b[:, 0:P], c, start=True, stop=True)
                made(pe.matmul(o[:, TOK:WIDE], b[:, P:TOK], c[:, P:TOK], start=True, stop=True), ("cb", g))

            def cum_row(h):
                o = open_bank(pe, ("cr", h))
                pe.matmul(o[:, 0:TOK], dtA[:, 0, h:h + 1].broadcast_to([P, P]), cst("triu"), start=True, stop=False)
                made(pe.matmul(o[:, P:TOK], dtA[:, 1, h:h + 1].broadcast_to([P, P]), cst("triu", 0, P),
                               start=False, stop=True), ("cr", h))

            cum_row(0)
            cum_row(1)
            project("g", 2, H)
            for pair in range(SSD_HEADS // 2):
                if pair in (2, 4, 6, 8, 10):
                    project("g", 2 + pair // 2, H)
                if pair + 1 < SSD_HEADS // 2:
                    cum_row(2 * pair + 2)
                    cum_row(2 * pair + 3)
                o = open_bank(pe, ("y", pair))
                if pair == 0:
                    for i in (4, 5, 6, 7):
                        wait_taken(pe, ("xs", i))
                for e in range(2):
                    h = 2 * pair + e
                    pe.wait_ge(S("ssd_w"), h + 1)
                    w = SEG[:, h % 4, :]
                    y = o[64 * e:64 * e + 64, :]
                    pe.matmul(y[:, 0:TOK], XDT[:, 0, 64 * h:64 * h + 64], w[:, 0:TOK], start=True, stop=False)
                    mm = pe.matmul(y[:, P:TOK], XDT[:, 1, 64 * h:64 * h + 64], w[:, TOK:WIDE], start=False, stop=True)
                made(mm, ("y", pair))
            pe.wait_ge(S("ya_ready"), 1)
            for t in range(4):
                project("attn", t, YA)
            for g in range(GROUPS):
                pe.wait_ge(S("ys_square"), 4 * (g + 1))
                sum_chunks(("gn", g), CONV[:, 4 * g:4 * g + 4, :], 4)
            for t in range(4):
                project("ssd", t, YS, 2, ready=None if t else lambda k: pe.wait_ge(S("ys_ready"), k + 1))
            for t in range(4):
                project("out", t, MIX, ready=None if t else taken_from("ssd"))

            sum_chunks("mean1", X, DC, ready=taken_from("out"))
            sum_chunks("var1", PROJ[:, 48:56, :], DC, ready=lambda k: pe.wait_ge(S("ln_square"), k + 1))

            def key_scores(t):
                if t == 0:
                    pe.wait_ge(S("sk_landed"), 16)
                wait_evacuated(pe, "query", t)
                for c in (2 * t, 2 * t + 1):
                    o = open_bank(pe, ("sc", c))
                    for u in range(TT):
                        mm = pe.matmul(o[:, u * P:(u + 1) * P], QT[:, c, u * P:(u + 1) * P], SK[:, c % 2, :],
                                       start=True, stop=True)
                    made(mm, ("sc", c))

            for t in range(8):
                project("query", t, H, ready=None if t else h_from(1))
                if t == 0:
                    for i in range(4):
                        o = open_bank(pe, ("h2", i))
                        t, q = i // 2, i % 2
                        for c in range(4):
                            mm = pe.transpose(o[:, c * P:(c + 1) * P], H[:, 4 * q + c, t * P:(t + 1) * P], ident)
                        made(mm, ("h2", i))
                else:
                    key_scores(t - 1)
            key_scores(7)

            pe.wait_ge(S("uv_used7"), 2 * 2 * NIT)
            for i in range(4):
                o = open_bank(pe, ("yt", i))
                for c in range(2):
                    for t in range(TT):
                        mm = pe.transpose(o[:, c * TOK + t * P:c * TOK + (t + 1) * P],
                                          YF[:, t, (2 * i + c) * P:(2 * i + c + 1) * P], ident)
                made(mm, ("yt", i))
            for i in range(4):
                wait_taken(pe, ("yt", i))
            sum_chunks("mean2", X, DC)
            sum_chunks("var2", PROJ[:, 48:56, :], DC, ready=lambda k: pe.wait_ge(S("ln_square"), DC + k + 1))

            def rms(job, k):
                sum_chunks(job, SQ2, DC, ready=lambda c: pe.wait_ge(S("rms_square"), DC * (k - 1) + c + 1))

            rms("rms_mix0", 1)
            def gate_products(c0):
                pe.wait_ge(S("xcv_sum"), c0 + 4)
                for c in range(c0, c0 + 4):
                    o = open_bank(pe, ("rg", c))
                    n, oc = c // 2, c % 2
                    for g in range(2):
                        for k in range(2):
                            mm = pe.matmul(o[:, g * TOK:(g + 1) * TOK], RGW[:, g, 2 * n + k, oc, :], XCV[:, 2 * n + k, :],
                                           start=(k == 0), stop=(k == 1))
                    made(mm, ("rg", c))

            for t in range(5):
                project("rec_in", t, H, ready=None if t else h_from(2))
            pe.wait_ge(S("rgw_landed"), 16)
            gate_products(0)
            project("rec_in", 5, H)
            gate_products(4)
            project("rec_in", 6, H)
            project("rec_in", 7, H)
            for t in range(4):
                project("rec_out", t, YR, ready=None if t else lambda k: pe.wait_ge(S("yr_ready"), k // 4 + 1))

            def mlp(layer):
                up, down = f"up{layer}", f"down{layer}"
                n0, t0 = COLT0[up], TILE0[up]
                with pe.Fori(0, 4) as i:
                    for s in range(4):
                        n = n0 + s
                        pe.wait_ge(S(f"pair_taken{n % 2}"), 2 * (n // 2) + i * 4)
                        pe.wait_ge(S(f"tile_landed{(t0 + s) % SLOTS}"), 16 * ((t0 + s) // SLOTS + 1) + i * 16)
                        w = ring[:, (t0 + s) % SLOTS, :].rearrange("p (k n) -> p k n", k=DC)
                        for c in range(2):
                            for k in range(DC):
                                mm = pe.matmul(acc(n, c), w[:, k, c * P:(c + 1) * P], H[:, k, :],
                                               start=(k == 0), stop=(k == DC - 1))
                        mm.then_inc(S(f"tile_used{(t0 + s) % SLOTS}"), 1)
                pe.wait_ge(S("hidden"), 32 * layer + 24 + 1)
                n0, t0 = COLT0[down], TILE0[down]
                with pe.Fori(0, 2) as i:
                    for half in range(2):
                        n = n0 + half
                        pe.wait_ge(S(f"pair_taken{n % 2}"), 2 * (n // 2) + i * 2)
                        for g in range(4):
                            s = t0 + 4 * half + g
                            if g == 3:
                                pe.wait_ge(S("hidden"), 32 * (layer + 1) + 1)
                            pe.wait_ge(S(f"tile_landed{s % SLOTS}"), 16 * (s // SLOTS + 1) + i * 32)
                            w = ring[:, s % SLOTS, :].rearrange("p (k n) -> p k n", k=DC)
                            for c in range(2):
                                for k in range(DC):
                                    mm = pe.matmul(acc(n, c), w[:, k, c * P:(c + 1) * P], HID[:, g * DC + k, :],
                                                   start=(g == 0 and k == 0), stop=(g == 3 and k == DC - 1))
                            mm.then_inc(S(f"tile_used{s % SLOTS}"), 1)

            rms("rms_mlp0", 2)
            pe.wait_ge(S("h_ready"), 4 * DC)
            mlp(0)

            o = open_bank(pe, "bv")
            pe.wait_ge(S("bias_consts_landed"), 48)
            made(pe.matmul(o[0:16, 0:WIDE], RELB, SELH, start=True, stop=True), "bv")
            rms("rms_mix1", 3)
            for t in range(3):
                project("att_in", t, H, ready=None if t else h_from(4))
            o = open_bank(pe, "wi")
            for t in range(TT):
                for k in range(DC):
                    mm = pe.matmul(o[:, 8 * t:8 * t + 8], H[:, k, t * P:(t + 1) * P], WWI[:, k, :],
                                   start=(k == 0), stop=(k == DC - 1))
            made(mm, "wi")
            o = open_bank(pe, "rms_c")
            pe.wait_ge(S("c_square"), 1)
            made(pe.matmul(o[:, 0:TOK], ones, TMP[:, 0:TOK], start=True, stop=True), "rms_c")
            project("att_in", 3, H)
            o = open_bank(pe, "ctok")
            pe.wait_ge(S("cn_ready"), 1)
            pe.transpose(o[:, 0:P], CN[:, 0:P], ident)
            made(pe.transpose(o[:, P:TOK], CN[:, P:TOK], ident), "ctok")
            wait_evacuated(pe, "att_in", 1)
            wait_evacuated(pe, "att_in", 2)
            for h in range(H_IDX):
                if h == H_IDX // 2:
                    project("att_in", 4, H)
                o = open_bank(pe, ("dot", h))
                a, b = 64 * (h % 2), 64 * (h % 2) + 64
                pe.matmul(o[:, 0:P], QI[a:b, h // 2, 0:P], KI[a:b, 0:P], start=True, stop=True)
                made(pe.matmul(o[:, P:WIDE], QI[a:b, h // 2, P:TOK], KI[a:b, :], start=True, stop=True), ("dot", h))
            project("att_in", 5, H)
            project("att_in", 6, H)
            wait_evacuated(pe, "att_in", 5)
            wait_evacuated(pe, "att_in", 6)
            s = TILE0["uk_uv"]
            pe.wait_ge(S(f"tile_landed{s % SLOTS}"), 16 * (s // SLOTS + 1))
            for h in range(H_ATT):
                o = open_bank(pe, ("ql", h))
                a, b = 64 * (h % 2), 64 * (h % 2) + 64
                made(pe.matmul(o[:, 0:TOK], UK[a:b, h // 2, :], QT2[a:b, h // 2, :], start=True, stop=True), ("ql", h))

            def logits(h):
                o = open_bank(pe, ("lg", h))
                if h == 0:
                    pe.wait_ge(S("bias_landed"), 32)
                    for i in range(12, 16):
                        wait_taken(pe, ("ql", i))
                pe.matmul(o[:, 0:WIDE], cst("flip"), BIAS[:, h, :], start=True, stop=False)
                pe.matmul(o[:, 0:P], QLAT[:, h, 0:P], CN[:, 0:P], start=False, stop=False)
                made(pe.matmul(o[:, P:WIDE], QLAT[:, h, P:TOK], CN, start=False, stop=True), ("lg", h))

            logits(0)
            logits(1)
            for h in range(H_ATT):
                if h + 2 < H_ATT:
                    logits(h + 2)
                o = open_bank(pe, ("pt", h))
                pe.wait_ge(S("p_ready"), h + 1)
                p = PR[h % 4]
                pe.transpose(o[:, 0:P], p[:, 0:P], ident)
                pe.transpose(o[:, P:2 * P], p[:, P:2 * P], ident)
                made(pe.transpose(o[:, 2 * P:3 * P], p[:, 2 * P:3 * P], ident), ("pt", h))
                o = open_bank(pe, ("ol", h))
                wait_taken(pe, ("pt", h))
                pt = PT[h % 2]
                pe.matmul(o[:, 0:TOK], CTOK[:, 0, :], pt[:, 0:TOK], start=True, stop=False)
                made(pe.matmul(o[:, P:TOK], CTOK[:, 1, :], pt[:, TOK:WIDE], start=False, stop=True), ("ol", h))
                if h % 2 == 1:
                    o = open_bank(pe, ("ot", h // 2))
                    for e in range(2):
                        wait_taken(pe, ("ol", h - 1 + e))
                        mm = pe.matmul(o[64 * e:64 * e + 64, 0:TOK], UVV[:, h - 1 + e, :], OL[(h - 1 + e) % 4],
                                       start=True, stop=True)
                    if h < H_ATT - 1:
                        made(mm, ("ot", h // 2))
                    else:
                        made(mm, ("ot", h // 2))
                        pe.wait_ge(S(f"job_made{JOBS[('ot', 7)] % 4}"), JOBS[("ot", 7)] // 4 + 1)
                        pe.sem_inc(S(f"tile_used{TILE0['uk_uv'] % SLOTS}"), 1)
            for t in range(4):
                project("att_out", t, OT, ready=None if t else lambda k: wait_taken(pe, ("ot", k)))
            rms("rms_mlp1", 4)
            pe.wait_ge(S("h_ready"), 6 * DC)
            mlp(1)
            rms("rms_fin", 5)

        @block.gpsimd
        def _(pool):
            pool.wait_ge(S("params_landed"), 32)
            for h in range(HEADS):
                slope = 2.0 ** (-8.0 * (h + 1) / HEADS)
                if h >= 2:
                    wait_taken(pool, ("s", h - 2, 1))
                pool.tensor_scalar(AB[h % 2], cst("dist"), -slope / DA_SCALE, 1.0, ALU.mult, ALU.mult)\
                    .then_inc(S("da_bias"), 1)

            for n in range(TT * SPT):
                b = n % NB
                if n % TOPK == 0:
                    pool.wait_ge(S("experts_ready"), n // TOPK + 1)
                if n >= NB:
                    pool.wait_ge(S(f"uv_used{b}"), n // NB)
                pool.indirect_dma_start(
                    out=UV[b], out_offset=None, in_=io["peer_uv"],
                    in_offset=bass.IndirectOffsetOnAxis(ap=EIDX[:, n // SPT, n % SPT:n % SPT + 1], axis=0),
                ).then_inc(S(f"uv_landed{b}"), 16)

        @block.scalar
        def _(act):
            st = Steps(act, "act_step")

            def on(*a, **k):
                st.did(act.activation(*a, **k))

            act.dma_start(rows[:, :], io["rows"]).then_inc(S("rows_landed"), 16)
            for s in range(SLOTS):
                act.dma_start(flat(adaW[:, s]), io["ada"][s]).then_inc(S(f"ada_landed{s}"), 16)
            for s in range(SLOTS):
                act.dma_start(flat(adaE[:, s]), io["ada"][SLOTS + s]).then_inc(S(f"ada_early{s}"), 16)
            act.dma_start(wdt[:, :, :], io["wdt"]).then_inc(S("wdt_landed"), 16)
            act.wait_ge(S("params_landed"), 32)
            act.activation(small[:, 240:248], pc("c", 0, 8), ACT.Silu).then_inc(S("c_ready"), 1)

            def ada_load(i):
                for s in range(SLOTS):
                    act.wait_ge(S("ada_tiles"), ada_done(i - 1 if i > 2 else 0, s))
                    act.dma_start(flat(adaW[:, s]), io["ada"][4 * i + s]).then_inc(S(f"ada_landed{s}"), 16)

            ada_load(2)
            act.wait_ge(S("h_ready"), DC)
            act.activation(X[:, :, :], X[:, :, :], ACT.Copy, scale=ALPHA).then_inc(S("x_scaled"), 1)
            act.wait_ge(S("lam_dots"), 2)
            act.activation(small[:, 18:20], small[:, 16:18], ACT.Exp).then_inc(S("lam_exp"), 1)

            def copy_out(name, t, dst):
                n = colt(name, t)
                wait_column(act, name, t)
                for c in range(2):
                    evacuated(act.activation(dst(c), acc(n, c), ACT.Copy), name, t)

            for t in range(4):
                copy_out("q", t, lambda c: Q[:, 2 * t + c, :])
            for t in range(4):
                copy_out("k", t, lambda c: K[:, 2 * t + c, :])
            for t in range(4):
                copy_out("v", t, lambda c: V[:, c, COLS * t:COLS * (t + 1)])

            def da_exp(h):
                act.wait_ge(S("da_negmax"), h + 1)
                for j in range(2):
                    for t in range(TT):
                        k = 2 * j + t
                        s = SC[h % 2][j][:, 0:P] if t == 0 else SC[h % 2][j][:, P:WIDE]
                        act.activation(s, s, ACT.Exp, bias=small[:, 8 * (h % 2) + k:8 * (h % 2) + k + 1],
                                       accum_out=small[:, 8 * (h % 2) + 4 + k:8 * (h % 2) + 5 + k]).then_inc(S("da_exp"), 1)

            dest = {"xbc": XBC, "z": Z, "g": G}
            def g_out(t):
                copy_out("g", t, lambda c: G[:, 2 * t + c, :])

            for h in range(HEADS):
                da_exp(h)
                if h in (1, 2, 3):
                    ada_load(h + 2)
                for name, t in beside_head(h):
                    copy_out(name, t, lambda c: dest[name][:, 2 * t + c, :])
                wait_made(act, ("t", h))
                taken(act.activation(AT[h % 2], bank(("t", h))[:, 0:WIDE], ACT.Copy), ("t", h))
                wait_made(act, ("o", h))
                taken(act.activation(YA[:, h, :], bank(("o", h))[:, 0:TOK], ACT.Copy), ("o", h))
                if h == 2:
                    act.wait_ge(S("rows_landed"), 16)
                    on(arow[:, 0, :], row("a_log"), ACT.Exp)
                    act.wait_ge(S("dt_negabs"), 1)
                    on(flat(dty), flat(dtx), ACT.Exp)
                    st.settle()
                    act.activation(flat(dtz), flat(dty), ACT.Ln, bias=1.0).then_inc(S("dt_ln"), 1)
            for h in range(HEADS):
                if h == 0:
                    wait_taken(act, ("o", 7))
                    wait_taken(act, ("o", 6))
                    g_out(0)
                act.activation(SQA(h), YA[:, h, :], ACT.Square).then_inc(S("da_square"), 1)
            for c in range(24):
                act.wait_ge(S("conv_sum"), c + 1)
                act.activation(CONV[:, c, :], CONV[:, c, :], ACT.Silu).then_inc(S("conv_ready"), 1)
            g_out(1)
            act.activation(Z[:, :, :], Z[:, :, :], ACT.Silu).then_inc(S("z_ready"), 1)
            act.wait_ge(S("da_var"), 1)
            act.activation(MIX[:, :, :], MIX[:, :, :], ACT.Sqrt).then_inc(S("da_rstd"), 1)
            g_out(2)
            for h in range(SSD_HEADS):
                if h % 4 == 0 and 4 <= h <= 20:
                    g_out(2 + h // 4)
                wait_taken(act, ("cr", h))
                act.activation(SEG[:, h % 4, :], SEG[:, h % 4, :], ACT.Exp).then_inc(S("decay_ready"), 1)
            for c in range(0, 16, 8):
                act.activation(G[:, c:c + 8, :], G[:, c:c + 8, :], ACT.Sigmoid).then_inc(S("g_ready"), 1)
            for c in range(16):
                act.wait_ge(S("ys_gated"), c + 1)
                act.activation(CONV[:, c, :], YS[:, c, :], ACT.Square).then_inc(S("ys_square"), 1)
            act.wait_ge(S("eps_set"), 1)
            for g in range(GROUPS):
                wait_made(act, ("gn", g))
                taken(act.activation(AUX[:, 28 + g, :], bank(("gn", g))[:, 0:TOK], ACT.Sqrt, scale=1.0 / 512, bias=EPS_COL), ("gn", g))

            def norm_help(k):
                for c in range(DC):
                    if c < DC - 1:
                        act.wait_ge(S("centered"), (DC - 1) * (k - 1) + c + 1)
                    else:
                        wait_taken(act, f"mean{k}")
                    act.activation(PROJ[:, 48 + c, :], H[:, c, :], ACT.Square).then_inc(S("ln_square"), 1)
                wait_made(act, f"var{k}")
                taken(act.activation(RS[:, :], bank(f"var{k}")[:, 0:TOK], ACT.Sqrt, scale=1.0 / D, bias=EPS_COL), f"var{k}")

            norm_help(1)
            act.dma_start(PROJ[:, 70, :], io["sk"]).then_inc(S("sk_landed"), 16)
            for c in range(DC):
                act.wait_ge(S("h_ready"), DC + c + 1)
                act.activation(X[:, c, :], X[:, c, :], ACT.Identity, scale=X_GAIN[:, c:c + 1], bias=X_SHIFT[:, c:c + 1])\
                    .then_inc(S("x_scaled"), 1)
            def score_out(t):
                for c in (2 * t, 2 * t + 1):
                    wait_made(act, ("sc", c))
                    taken(act.activation(SCO[:, :, c, :], bank(("sc", c))[:, 0:TOK].rearrange("p (t n) -> p t n", t=TT),
                                         ACT.Copy), ("sc", c))

            for t in range(8):
                copy_out("query", t, lambda c: QT[:, 2 * t + c, :])
                if t == 0:
                    for i in range(4):
                        wait_made(act, ("h2", i))
                        taken(act.activation(H2T[:, i // 2, 512 * (i % 2):512 * (i % 2) + 512], bank(("h2", i)), ACT.Copy),
                              ("h2", i))
                if t:
                    score_out(t - 1)
            score_out(7)
            act.activation(GEL[:, 0:1], par[:, 0:1], ACT.Copy).then_inc(S("weight_ready"), 1)
            for tt in range(TT):
                act.wait_ge(S("top_shifted"), tt + 1)
                act.activation(GT[:, tt], GT[:, tt], ACT.Exp).then_inc(S("top_exp"), 1)
                with act.Fori(0, NIT) as i:
                    for k in range(BODY):
                        n = tt * SPT + k
                        act.wait_ge(S("dot_ready"), n + 1 + i * BODY)
                        act.activation(GEL[:, k:k + 1], DOT[:, k:k + 1], ACT.Gelu).then_inc(S("gelu_ready"), 1)
                        act.wait_ge(S("gelu_ready"), n + 1 + i * BODY)
                        act.activation(W16[:, k:k + 1], GEL[:, k:k + 1], ACT.Copy, scale=G16[:, k:k + 1])\
                            .then_inc(S("weight_ready"), 1)
            for b in range(NB):
                act.wait_ge(S(f"uv_used{b}"), 2 * 2 * NIT)
            act.dma_start(flat(CONV[:, 0:16, :]), io["rgw"]).then_inc(S("rgw_landed"), 16)
            act.dma_start(WWI[:, :, :], io["wwi"]).then_inc(S("bias_consts_landed"), 16)
            act.dma_start(SELH, io["selh"]).then_inc(S("bias_consts_landed"), 16)
            act.dma_start(RELB, io["relb"]).then_inc(S("bias_consts_landed"), 16)
            norm_help(2)

            def rms_help(job, last=None):
                for c in range(DC):
                    if last:
                        n = colt(last, c // 2)
                        act.wait_ge(S(f"pair_taken{n % 2}"), 2 * (n // 2) + c % 2 + 1)
                    else:
                        act.wait_ge(S("x_ready"), c + 1)
                    act.activation(SQ2[:, c, :], X[:, c, :], ACT.Square).then_inc(S("rms_square"), 1)
                wait_made(act, job)
                taken(act.activation(RS[:, :], bank(job)[:, 0:TOK], ACT.Sqrt, scale=1.0 / D, bias=EPS2_COL), job)

            act.wait_ge(S("lam_negabs"), 1)
            on(RGC[:, 8:16], RGC[:, 0:8], ACT.Exp)
            st.settle()
            act.activation(RGC[:, 0:8], RGC[:, 8:16], ACT.Ln, bias=1.0).then_inc(S("lam_ln"), 1)
            rms_help("rms_mix0")
            def rec_gate_out(t):
                n = colt("rec_in", t)
                wait_column(act, "rec_in", t)
                for c in range(2):
                    evacuated(act.activation(GATE[:, 2 * (t - 4) + c, :], acc(n, c), ACT.Gelu_apprx_tanh), "rec_in", t)

            def sigmoids(c0):
                for c in range(c0, c0 + 4):
                    wait_made(act, ("rg", c))
                    b = bank(("rg", c))
                    on(RR[:, c, :], b[:, 0:TOK], ACT.Sigmoid, bias=pc("rec_b_a", c))
                    taken(act.activation(II[:, c, :], b[:, TOK:2 * TOK], ACT.Sigmoid, bias=pc("rec_b_x", c)), ("rg", c))

            for t in range(4):
                copy_out("rec_in", t, lambda c: XR[:, 2 * t + c, :])
            rec_gate_out(4)
            sigmoids(0)
            rec_gate_out(5)
            sigmoids(4)
            for c in (0, 4):
                act.wait_ge(S("log_a"), c + 4)
                on(AA[:, c:c + 4, :], RR[:, c:c + 4, :], ACT.Exp)
                act.activation(RR[:, c:c + 4, :], RR[:, c:c + 4, :], ACT.Tanh).then_inc(S("a_ready"), 1)
            rec_gate_out(6)
            for c in (0, 4):
                act.wait_ge(S("u_square"), c // 4 + 1)
                act.activation(T1[:, c:c + 4, :], T1[:, c:c + 4, :], ACT.Sqrt, scale=-1.0).then_inc(S("u_root"), 1)
            rec_gate_out(7)
            rms_help("rms_mlp0", "rec_out")

            def mlp(layer):
                up = f"up{layer}"
                n0, t0 = COLT0[up], TILE0[up]
                with act.Fori(0, 4) as i:
                    for s in range(4):
                        act.wait_ge(S(f"tile_used{(t0 + s) % SLOTS}"), (t0 + s) // SLOTS + 1 + i)
                        for c in range(2):
                            act.wait_ge(S("hidden"), 32 * layer + 1 + i * 8)
                            act.activation(RL[2 * s + c], acc(n0 + s, c), ACT.Relu)\
                                .then_inc(S(f"pair_taken{(n0 + s) % 2}"), 1)

            mlp(0)
            wait_made(act, "bv")
            taken(act.activation(BVS[:, 0:WIDE], bank("bv")[0:16, 0:WIDE], ACT.Copy), "bv")
            wait_taken(act, "bv")
            act.dma_start(io["bv"], BVS[:, 0:WIDE]).then_inc(S("bv_stored"), 16)
            act.wait_ge(S("bv_stored"), 16)
            bv = io["bv"]
            for q, a, b in ((0, 0, P), (1, P, WIDE)):
                src = bass.AP(tensor=bv.tensor, offset=bv.offset + P - P * q, ap=[[1, P], [WIDE, H_ATT], [1, b - a]])
                act.dma_start(BIAS[:, :, a:b], src).then_inc(S("bias_landed"), 16)
            rms_help("rms_mix1", "down0")
            def att_q_out(t):
                copy_out("att_in", t, lambda c: QT2[:, 2 * (t - 3) + c, :])

            copy_out("att_in", 0, lambda c: (CR, QI[:, 0, :])[c])
            wait_evacuated(act, "att_in", 0)
            act.activation(TMP[:, 0:TOK], CR, ACT.Square).then_inc(S("c_square"), 1)
            copy_out("att_in", 1, lambda c: QI[:, 1 + c, :])
            copy_out("att_in", 2, lambda c: (QI[:, 3, :], KI)[c])
            wait_made(act, "rms_c")
            taken(act.activation(RS[:, :], bank("rms_c")[:, 0:TOK], ACT.Sqrt, scale=1.0 / P, bias=EPS2_COL), "rms_c")
            att_q_out(3)
            wait_made(act, "ctok")
            taken(act.activation(CTOK[:, :, :], bank("ctok")[:, 0:TOK].rearrange("p (t c) -> p t c", t=TT), ACT.Copy), "ctok")
            for t in (4, 5, 6):
                att_q_out(t)
            for h in range(H_ATT):
                wait_made(act, ("ql", h))
                taken(act.activation(QLAT[:, h, :], bank(("ql", h))[:, 0:TOK], ACT.Copy, scale=ATT_SCALE), ("ql", h))

            def att_exp(h):
                act.wait_ge(S("lg_negmax"), h + 1)
                for t in range(TT):
                    p = PR[h % 4][:, 0:P] if t == 0 else PR[h % 4][:, P:WIDE]
                    k = 2 * (h % 4) + t
                    act.activation(p, p, ACT.Exp, bias=MX[:, k:k + 1], accum_out=SM[:, k:k + 1]).then_inc(S("lg_exp"), 1)

            att_exp(0)
            for h in range(H_ATT):
                if h + 1 < H_ATT:
                    att_exp(h + 1)
                wait_made(act, ("pt", h))
                taken(act.activation(PT[h % 2], bank(("pt", h))[:, 0:WIDE], ACT.Copy), ("pt", h))
                wait_made(act, ("ol", h))
                taken(act.activation(OL[h % 4], bank(("ol", h))[:, 0:TOK], ACT.Copy), ("ol", h))
                if h % 2 == 1:
                    wait_made(act, ("ot", h // 2))
                    taken(act.activation(OT[:, h // 2, :], bank(("ot", h // 2))[:, 0:TOK], ACT.Copy), ("ot", h // 2))
            rms_help("rms_mlp1", "att_out")
            mlp(1)
            rms_help("rms_fin", "down1")

        @block.vector
        def _(dve):
            st = Steps(dve, "dve_step")
            did, settle = st.did, st.settle
            cc = small[:, 240:248]

            def ada(i, base):
                w = adaE if i == 1 else adaW
                for pair in (0, 2):
                    for s in (pair, pair + 1):
                        if i == 1:
                            dve.wait_ge(S(f"ada_early{s}"), 16)
                        else:
                            dve.wait_ge(S(f"ada_landed{s}"), 16 * max(i, 1))
                    for k in range(DC):
                        for s in (pair, pair + 1):
                            o = CONV[:, base + s, :]
                            if k:
                                dve.wait_ge(S("ada_tiles"), ada_done(i, s) - 2 * (DC - k))
                                ins = dve.scalar_tensor_tensor(o, w[:, s, k, :], cc[:, k:k + 1], o, ALU.mult, ALU.add)
                            else:
                                ins = dve.tensor_scalar(o, w[:, s, 0, :], cc[:, 0:1], None, ALU.mult)
                            ins.then_inc(S("ada_tiles"), 1)

            did(dve.memset(EPS_COL, EPS))
            dve.memset(EPS2_COL, EPS_2).then_inc(S("eps_set"), 1)
            dve.wait_ge(S("c_ready"), 1)
            ada(0, 16)
            ada(1, 20)
            wait_made(dve, "mod_a")
            taken(dve.tensor_tensor(mod[:, 0:16], bank("mod_a")[:, 0:16], pc("b_ada", 0, 16), ALU.add), "mod_a")
            wait_taken(dve, "mod_a")
            did(dve.tensor_scalar(mod[:, 8:16], mod[:, 8:16], 1.0, None, ALU.add))
            settle()
            dve.wait_ge(S("x_landed"), 16)
            for c in range(DC):
                dve.tensor_scalar(H[:, c, :], X[:, c, :], mod[:, 8 + c:9 + c], mod[:, c:c + 1], ALU.mult, ALU.add)\
                    .then_inc(S("h_ready"), 1)
            dve.wait_ge(S("rows_landed"), 16)
            for i in (1, 2):
                q, k = row(f"lambda_q{i}"), row(f"lambda_k{i}")
                dve.tensor_tensor_reduce(q, q, k, 1.0, 0.0, ALU.mult, ALU.add, small[:, 15 + i:16 + i])\
                    .then_inc(S("lam_dots"), 1)

            def da_scores(h):
                dve.wait_ge(S("da_bias"), h + 1)
                m = small[:, 8 * (h % 2):8 * (h % 2) + 4]
                for j in range(2):
                    wait_made(dve, ("s", h, j))
                    b = bank(("s", h, j))
                    if j == 0 and h >= 2:
                        dve.wait_ge(S("da_diff"), h - 1)
                    for t, (x, y) in enumerate(((0, P), (P, WIDE))):
                        ins = dve.tensor_tensor_reduce(SC[h % 2][j][:, x:y], b[:, x:y], AB[h % 2][:, x:y], DA_SCALE, NEG,
                                                       ALU.add, ALU.max, m[:, 2 * j + t:2 * j + t + 1])
                        if t:
                            taken(ins, ("s", h, j))
                        else:
                            did(ins)
                wait_taken(dve, ("s", h, 0))
                wait_taken(dve, ("s", h, 1))
                dve.tensor_scalar(m, m, -1.0, None, ALU.mult).then_inc(S("da_negmax"), 1)

            def da_combine(h):
                dve.wait_ge(S("da_exp"), 4 * (h + 1))
                sums = small[:, 8 * (h % 2) + 4:8 * (h % 2) + 8]
                did(dve.reciprocal(sums, sums))
                settle()
                did(dve.tensor_scalar(sums[:, 2:4], sums[:, 2:4], small[:, 20:21], None, ALU.mult))
                settle()
                if h >= 2:
                    wait_made(dve, ("t", h - 2))
                for t, (x, y) in enumerate(((0, P), (P, WIDE))):
                    did(dve.tensor_scalar(AM[h % 2][:, x:y], SC[h % 2][0][:, x:y], sums[:, t:t + 1], None, ALU.mult))
                settle()
                for t, (x, y) in enumerate(((0, P), (P, WIDE))):
                    ins = dve.scalar_tensor_tensor(AM[h % 2][:, x:y], SC[h % 2][1][:, x:y], sums[:, 2 + t:3 + t],
                                                   AM[h % 2][:, x:y], ALU.mult, ALU.add)
                    if t:
                        ins.then_inc(S("da_diff"), 1)
                    else:
                        did(ins)

            def conv(c0, n, src, w, b, chunks, dst, sem):
                for k in (3, 2, 1, 0):
                    d = 3 - k
                    if d:
                        settle()
                    for c in range(c0, c0 + n):
                        o, x, wk = dst[:, c, :], src[:, c, :], pc(w, k * chunks + c)
                        if d == 0:
                            did(dve.tensor_scalar(o, x, wk, pc(b, c), ALU.mult, ALU.add))
                            continue
                        ins = dve.scalar_tensor_tensor(o[:, d:TOK], x[:, 0:TOK - d], wk, o[:, d:TOK], ALU.mult, ALU.add)
                        if k:
                            did(ins)
                        else:
                            ins.then_inc(S(sem), 1)

            for h in range(HEADS):
                da_scores(h)
                if h == 0:
                    dve.wait_ge(S("lam_exp"), 1)
                    did(dve.scalar_tensor_tensor(small[:, 20:21], small[:, 19:20], -LAMBDA_INIT, small[:, 18:19],
                                                 ALU.add, ALU.subtract))
                    settle()
                if h == 1:
                    dve.wait_ge(S("rows_landed"), 16)
                    wait_made(dve, "dt")
                    taken(dve.tensor_tensor(dt_[:, :, :], bank("dt")[:, 0:64].rearrange("p (t n) -> p t n", t=TT),
                                            over(row("dt_bias"), TT), ALU.add), "dt")
                    wait_taken(dve, "dt")
                    dve.scalar_tensor_tensor(flat(dtx), flat(dt_), -1.0, flat(dt_), ALU.mult, ALU.min).then_inc(S("dt_negabs"), 1)
                if h < 4:
                    ada(2 + h, 4 * h)
                da_combine(h)
                if h == 3:
                    dve.wait_ge(S("dt_ln"), 1)
                    did(dve.scalar_tensor_tensor(flat(dt_), flat(dt_), 0.0, flat(dtz), ALU.max, ALU.add))
                    settle()
                    dve.scalar_tensor_tensor(dtA[:, :, :], dt_[:, :, :], -1.0, over(arow[:, 0, :], TT), ALU.mult, ALU.mult)\
                        .then_inc(S("dta_ready"), 1)
                if h == 4:
                    wait_made(dve, "mod_b")
                    taken(dve.tensor_tensor(mod[:, 16:48], bank("mod_b")[:, 0:32], pc("b_ada", 16, 32), ALU.add), "mod_b")
                    wait_taken(dve, "mod_b")
                    did(dve.tensor_scalar(mod[:, 32:40], mod[:, 32:40], 1.0, None, ALU.add))
                    settle()
                    g, b = pc("ln1_g", 0, DC), pc("ln1_b", 0, DC)
                    did(dve.tensor_tensor(H_GAIN, g, mod[:, 32:40], ALU.mult))
                    did(dve.tensor_tensor(H_SHIFT, b, mod[:, 32:40], ALU.mult))
                    did(dve.tensor_scalar(X_GAIN, g, ALPHA, None, ALU.mult))
                    did(dve.tensor_scalar(X_SHIFT, b, ALPHA, None, ALU.mult))
                    settle()
                    did(dve.tensor_tensor(H_SHIFT, H_SHIFT, mod[:, 24:32], ALU.add))
                    for t in range(TT):
                        wait_made(dve, f"cum{t}")
                        taken(dve.tensor_copy(cum[:, t, :], bank(f"cum{t}")[:, 0:32]), f"cum{t}")
                        wait_taken(dve, f"cum{t}")
                if 4 <= h < 7:
                    for t in range(4 * (h - 4), 4 * (h - 4) + 4):
                        wait_evacuated(dve, "xbc", t)
                    conv(8 * (h - 4), 8, XBC, "conv_w", "conv_b", 24, CONV, "conv_sum")

            for h in range(HEADS):
                wait_made(dve, ("yn", h))
                taken(dve.tensor_scalar(MIX[:, h, :], bank(("yn", h))[:, 0:TOK], 1.0 / P, EPS, ALU.mult, ALU.add), ("yn", h))
            for h in range(4, 8):
                wait_taken(dve, ("yn", h))
            dve.reciprocal(MIX[:, :, :], MIX[:, :, :]).then_inc(S("da_var"), 1)
            did(dve.tensor_scalar(small[:, 21:22], pc("subln"), 1.0 - LAMBDA_INIT, None, ALU.mult))
            for i in range(8):
                wait_made(dve, ("xs", i))
                t, q = i % 2, i // 2
                taken(dve.tensor_tensor(XDT[:, t, 512 * q:512 * q + 512].rearrange("p (h n) -> p h n", n=64),
                                        bank(("xs", i)).rearrange("p (h n) -> p h n", n=64),
                                        dt_[:, t, 8 * q:8 * q + 8].rearrange("p (h o) -> p h o", o=1).broadcast_to([P, 8, 64]),
                                        ALU.mult), ("xs", i))
            for g in range(GROUPS):
                wait_made(dve, ("cb", g))
                b = bank(("cb", g))
                did(dve.tensor_tensor(CB[:, g, 0:TOK], b[:, 0:TOK], cst("triu"), ALU.mult))
                taken(dve.tensor_tensor(CB[:, g, TOK:WIDE], b[:, TOK:WIDE], cst("triu", 0, P), ALU.mult), ("cb", g))
            settle()
            for g in range(GROUPS):
                wait_taken(dve, ("cb", g))
            dve.wait_ge(S("da_rstd"), 1)
            dve.scalar_tensor_tensor(YA[:, :, :], YA[:, :, :], small[:, 21:22], MIX[:, :, :], ALU.mult, ALU.mult)\
                .then_inc(S("ya_ready"), 1)

            def segment(h):
                wait_made(dve, ("cr", h))
                b = bank(("cr", h))
                if h >= 4:
                    wait_made(dve, ("y", (h - 4) // 2))
                did(dve.tensor_scalar(SEG[:, h % 4, 0:TOK], b[:, 0:TOK], cum[:, 0, h:h + 1], 0.0, ALU.subtract, ALU.min))
                taken(dve.tensor_scalar(SEG[:, h % 4, TOK:WIDE], b[:, P:TOK], cum[:, 1, h:h + 1], 0.0,
                                        ALU.subtract, ALU.min), ("cr", h))

            def weigh(h):
                dve.wait_ge(S("decay_ready"), h + 1)
                dve.tensor_tensor(SEG[:, h % 4, :], SEG[:, h % 4, :], CB[:, h // 8, :], ALU.mult).then_inc(S("ssd_w"), 1)

            def gate_out(pair):
                wait_made(dve, ("y", pair))
                taken(dve.scalar_tensor_tensor(YS[:, pair, :], CONV[:, pair, :], pc("d_skip", pair), bank(("y", pair))[:, 0:TOK],
                                               ALU.mult, ALU.add), ("y", pair))
                wait_taken(dve, ("y", pair))
                if pair == 0:
                    dve.wait_ge(S("z_ready"), 1)
                dve.tensor_tensor(YS[:, pair, :], YS[:, pair, :], Z[:, pair, :], ALU.mult).then_inc(S("ys_gated"), 1)

            segment(0)
            segment(1)
            for pair in range(SSD_HEADS // 2):
                if pair >= 1:
                    gate_out(pair - 1)
                if pair + 1 < SSD_HEADS // 2:
                    segment(2 * pair + 2)
                weigh(2 * pair)
                if pair + 1 < SSD_HEADS // 2:
                    segment(2 * pair + 3)
                weigh(2 * pair + 1)
            gate_out(SSD_HEADS // 2 - 1)

            dve.wait_ge(S("g_ready"), 2)
            for t in range(4):
                n = colt("attn", t)
                wait_column(dve, "attn", t)
                for c in range(2):
                    k = 2 * t + c
                    evacuated(dve.tensor_tensor(MIX[:, k, :], acc(n, c), G[:, k, :], ALU.mult), "attn", t)
            for g in range(GROUPS):
                wait_taken(dve, ("gn", g))
                did(dve.reciprocal(AUX[:, 28 + g, :], AUX[:, 28 + g, :]))
                settle()
                for k in range(4 * g, 4 * g + 4):
                    dve.scalar_tensor_tensor(YS[:, k, :], YS[:, k, :], pc("ssd_norm_w", k), AUX[:, 28 + g, :], ALU.mult, ALU.mult)\
                        .then_inc(S("ys_ready"), 1)
                dve.wait_ge(S("ys_ready"), 4 * (g + 1))
            for t in range(4):
                n = colt("ssd", t)
                wait_column(dve, "ssd", t, 2)
                for c in range(2):
                    k = 2 * t + c
                    did(dve.tensor_tensor(G[:, k, :], acc(n, c), G[:, 8 + k, :], ALU.mult))
                settle()
                for c in range(2):
                    k = 2 * t + c
                    evacuated(dve.tensor_tensor(MIX[:, k, :], MIX[:, k, :], G[:, k, :], ALU.add), "ssd", t)
            dve.wait_ge(S("x_scaled"), 1)
            for t in range(4):
                n = colt("out", t)
                wait_column(dve, "out", t)
                for c in range(2):
                    k = 2 * t + c
                    evacuated(dve.scalar_tensor_tensor(X[:, k, :], acc(n, c), mod[:, 16 + k:17 + k], X[:, k, :],
                                                       ALU.mult, ALU.add), "out", t)

            def center(i):
                wait_made(dve, f"mean{i}")
                for c in range(DC):
                    ins = dve.scalar_tensor_tensor(H[:, c, :], bank(f"mean{i}")[:, 0:TOK], -1.0 / D, X[:, c, :], ALU.mult, ALU.add)
                    if c < DC - 1:
                        ins.then_inc(S("centered"), 1)
                    else:
                        taken(ins, f"mean{i}")
                wait_taken(dve, f"mean{i}")
                wait_taken(dve, f"var{i}")
                did(dve.reciprocal(RS[:, :], RS[:, :]))
                settle()

            center(1)
            for c in range(DC):
                dve.tensor_tensor(X[:, c, :], H[:, c, :], RS[:, :], ALU.mult).then_inc(S("x_normed"), 1)
                if c:
                    dve.wait_ge(S("x_normed"), c)
                    dve.tensor_scalar(H[:, c - 1, :], X[:, c - 1, :], H_GAIN[:, c - 1:c], H_SHIFT[:, c - 1:c], ALU.mult, ALU.add)\
                        .then_inc(S("h_ready"), 1)
            dve.wait_ge(S("x_normed"), DC)
            dve.tensor_scalar(H[:, DC - 1, :], X[:, DC - 1, :], H_GAIN[:, DC - 1:DC], H_SHIFT[:, DC - 1:DC], ALU.mult, ALU.add)\
                .then_inc(S("h_ready"), 1)

            def top16(rows_, vals, idx):
                for half in (0, 8):
                    for r, v in zip(rows_, vals):
                        did(dve.max(v[:, half:half + 8], r))
                    settle()
                    for r, v, x in zip(rows_, vals, idx):
                        did(dve.max_index(x[:, half:half + 8], v[:, half:half + 8], r))
                    settle()
                    if half == 0:
                        for r, v in zip(rows_, vals):
                            did(dve.match_replace(r, v[:, 0:8], r, NEG))
                        settle()

            def pick(t, h):
                cs = (2 * h, 2 * h + 1)
                top16([SCO[:, t, c, :] for c in cs], [TV[:, t, c, :] for c in cs], [TI[:, t, c, :] for c in cs])
                did(dve.tensor_copy(TIF[:, t, 2 * h:2 * h + 2, :], TI[:, t, 2 * h:2 * h + 2, :]))
                cand = CAND[:, t, 256 * h:256 * h + 256]
                did(dve.tensor_tensor(cand.rearrange("p (a b) -> p a b", a=TOPK),
                                      TV[:, t, 2 * h, :].rearrange("p (k o) -> p k o", o=1).broadcast_to([P, TOPK, TOPK]),
                                      over(TV[:, t, 2 * h + 1, :], TOPK), ALU.add))
                settle()
                top16([cand], [TS[:, t, h, :]], [TP[:, t, h, :]])
                did(dve.tensor_scalar(RANK[:, 0, :], TP[:, t, h, :], 4, None, ALU.logical_shift_right))
                did(dve.tensor_scalar(RANK[:, 1, :], TP[:, t, h, :], 15, None, ALU.bitwise_and))
                settle()
                did(dve.tensor_copy(RANKF, RANK))
                settle()
                did(dve.tensor_tensor(HOT, each(RANKF, TOPK),
                                      cst("iota").rearrange("p (o q k) -> p o q k", o=1, q=1).broadcast_to([P, 2, TOPK, TOPK]),
                                      ALU.is_equal))
                settle()
                did(dve.tensor_tensor(HOT, HOT, TIF[:, t, 2 * h:2 * h + 2, :].rearrange("p j (o k) -> p j o k", o=1)
                                      .broadcast_to([P, 2, TOPK, TOPK]), ALU.mult))
                settle()
                did(dve.tensor_reduce(KEYS, HOT, AX.X, ALU.add))
                settle()
                did(dve.scalar_tensor_tensor(KEYS[:, 1, :], KEYS[:, 0, :], 128.0, KEYS[:, 1, :], ALU.mult, ALU.add))
                settle()
                dve.tensor_copy(EIDX[:, t, 16 * h:16 * h + 16], KEYS[:, 1, :]).then_inc(S("experts_ready"), 1)

            def gates(t):
                ts, gt = TS[:, t], GT[:, t]
                dve.tensor_tensor(gt, ts, ts[:, :, 0:1].broadcast_to([P, HEADS, TOPK]), ALU.subtract)\
                    .then_inc(S("top_shifted"), 1)
                dve.wait_ge(S("top_exp"), t + 1)
                did(dve.tensor_reduce(GS_, gt, AX.X, ALU.add))
                settle()
                did(dve.reciprocal(GS_, GS_))
                settle()
                did(dve.tensor_tensor(gt, gt, GS_.rearrange("p (a o) -> p a o", o=1).broadcast_to([P, HEADS, TOPK]), ALU.mult))
                settle()

            did(dve.memset(YF.rearrange("p t n -> p (t n)"), 0.0))
            for h in range(HEADS):
                wait_taken(dve, ("sc", 2 * h))
                wait_taken(dve, ("sc", 2 * h + 1))
                pick(0, h)
            gates(0)
            for i in range(4):
                wait_taken(dve, ("h2", i))
            gflat = GT.rearrange("p t h k -> p t (h k)")

            def slots(tt, i):
                n0 = tt * SPT

                def add_value(k):
                    b = k % NB
                    dve.wait_ge(S("weight_ready"), n0 + k + 2 + i * BODY)
                    if k:
                        dve.wait_ge(S(f"uv_used{(k - 1) % NB}"), tt * 2 * NIT + (k - 1) // NB + 1 + i * 2)
                    dve.scalar_tensor_tensor(YF[:, tt, :], UV[b][:, D:2 * D], W16[:, k:k + 1], YF[:, tt, :],
                                             ALU.mult, ALU.add).then_inc(S(f"uv_used{b}"), 1)

                dve.wait_ge(S("weight_ready"), n0 + 1 + i * BODY)
                g = gflat[:, tt, i * BODY:(i + 1) * BODY] if isinstance(i, int) else gflat[:, tt, bass.ds(i * BODY, BODY)]
                dve.tensor_copy(G16, g).then_inc(S("slot_gates"), 1)
                dve.wait_ge(S("slot_gates"), tt * NIT + 1 + i)
                for k in range(BODY):
                    b, use = k % NB, tt * 2 * NIT + k // NB + 1
                    dve.wait_ge(S(f"uv_landed{b}"), 16 * use + i * 32)
                    if k:
                        dve.wait_ge(S("dot_ready"), n0 + k + i * BODY)
                    dve.tensor_tensor_reduce(PRODS[k % 2], UV[b][:, 0:D], H2T[:, tt, :], 1.0, 0.0, ALU.mult, ALU.add,
                                             DOT[:, k:k + 1]).then_inc(S("dot_ready"), 1)
                    if k:
                        add_value(k - 1)
                add_value(BODY - 1)

            for h in range(HEADS):
                slots(0, h)
                pick(1, h)
            gates(1)
            with dve.Fori(0, NIT) as i:
                slots(1, i)

            dve.wait_ge(S("x_scaled"), 1 + DC)
            for i in range(4):
                wait_made(dve, ("yt", i))
                for c in range(2):
                    k = 2 * i + c
                    ins = dve.scalar_tensor_tensor(X[:, k, :], bank(("yt", i))[:, c * TOK:(c + 1) * TOK],
                                                   mod[:, 40 + k:41 + k], X[:, k, :], ALU.mult, ALU.add)
                    if c:
                        taken(ins, ("yt", i))
                    else:
                        did(ins)
            settle()
            center(2)
            for c in range(DC):
                dve.tensor_tensor(X[:, c, :], H[:, c, :], RS[:, :], ALU.mult).then_inc(S("x_normed"), 1)
                if c:
                    dve.wait_ge(S("x_normed"), DC + c)
                    dve.tensor_scalar(X[:, c - 1, :], X[:, c - 1, :], pc("ln2_g", c - 1), pc("ln2_b", c - 1), ALU.mult, ALU.add)\
                        .then_inc(S("x_ready"), 1)
            dve.wait_ge(S("x_normed"), 2 * DC)
            dve.tensor_scalar(X[:, DC - 1, :], X[:, DC - 1, :], pc("ln2_g", DC - 1), pc("ln2_b", DC - 1), ALU.mult, ALU.add)\
                .then_inc(S("x_ready"), 1)
            dve.wait_ge(S("x_ready"), DC)

            def rms_norm(job, g, g0, out_sem="h_ready"):
                wait_taken(dve, job)
                did(dve.reciprocal(RS[:, :], RS[:, :]))
                settle()
                for c in range(DC):
                    dve.scalar_tensor_tensor(H[:, c, :], X[:, c, :], pc(g, g0 + c), RS[:, :], ALU.mult, ALU.mult)\
                        .then_inc(S(out_sem), 1)

            dve.scalar_tensor_tensor(RGC[:, 0:8], pc("rec_lambda", 0, 8), -1.0, pc("rec_lambda", 0, 8), ALU.mult, ALU.min).then_inc(S("lam_negabs"), 1)
            did(dve.tensor_scalar(small[:, 232:240], pc("rec_lambda", 0, 8), 0.0, None, ALU.min))
            dve.wait_ge(S("lam_ln"), 1)
            settle()
            did(dve.scalar_tensor_tensor(RGC[:, 0:8], RGC[:, 0:8], -1.0, small[:, 232:240], ALU.mult, ALU.add))
            settle()
            did(dve.tensor_scalar(RGC[:, 0:8], RGC[:, 0:8], RG_C, None, ALU.mult))
            rms_norm("rms_mix0", "mix_g", 0)
            for c in (0, 4):
                wait_evacuated(dve, "rec_in", c // 2)
                wait_evacuated(dve, "rec_in", c // 2 + 1)
                conv(c, 4, XR, "rec_conv_w", "rec_conv_b", 8, XCV, "xcv_sum")
            halves_ = [slice(0, 4), slice(4, 8)]
            for i, hs in enumerate(halves_):
                for c in range(4 * i, 4 * i + 4):
                    wait_taken(dve, ("rg", c))
                    dve.tensor_scalar(RR[:, c, :], RR[:, c, :], RGC[:, c:c + 1], None, ALU.mult).then_inc(S("log_a"), 1)
                did(dve.tensor_tensor(XCV[:, hs, :], XCV[:, hs, :], II[:, hs, :], ALU.mult))
            for i, hs in enumerate(halves_):
                dve.wait_ge(S("a_ready"), i + 1)
                did(dve.tensor_tensor(T1[:, hs, :], AA[:, hs, :], AA[:, hs, :], ALU.mult))
                settle()
                dve.scalar_tensor_tensor(T1[:, hs, :], T1[:, hs, :], 1.0, RR[:, hs, :], ALU.add, ALU.mult)\
                    .then_inc(S("u_square"), 1)
            for i, hs in enumerate(halves_):
                dve.wait_ge(S("u_root"), i + 1)
                did(dve.tensor_tensor(T1[:, hs, :], T1[:, hs, :], XCV[:, hs, :], ALU.mult))
                settle()
                for c in range(4 * i, 4 * i + 4):
                    did(dve.tensor_tensor_scan(YR[:, c, :], AA[:, c, :], T1[:, c, :], 0.0, ALU.mult, ALU.add))
                settle()
                for t in (4 + 2 * i, 5 + 2 * i):
                    wait_evacuated(dve, "rec_in", t)
                dve.tensor_tensor(YR[:, hs, :], YR[:, hs, :], GATE[:, hs, :], ALU.mult).then_inc(S("yr_ready"), 1)

            def residual(name):
                for t in range(4):
                    n = colt(name, t)
                    wait_column(dve, name, t)
                    for c in range(2):
                        k = 2 * t + c
                        evacuated(dve.tensor_tensor(X[:, k, :], acc(n, c), X[:, k, :], ALU.add), name, t)
                wait_evacuated(dve, name, 2)
                wait_evacuated(dve, name, 3)

            def mlp(layer):
                up, down = f"up{layer}", f"down{layer}"
                n0 = COLT0[up]
                with dve.Fori(0, 4) as i:
                    for s in range(4):
                        n = n0 + s
                        for c in range(2):
                            dve.wait_ge(S(f"pair_taken{n % 2}"), 2 * (n // 2) + c + 1 + i * 4)
                            r = RL[2 * s + c]
                            dve.tensor_tensor(HID[:, bass.ds(8 * i + (2 * s + c), 1), :].rearrange("p o n -> p (o n)"), r, r,
                                              ALU.mult).then_inc(S("hidden"), 1)
                n0, t0 = COLT0[down], TILE0[down]
                with dve.Fori(0, 2) as i:
                    for half in range(2):
                        n = n0 + half
                        s = t0 + 4 * half + 3
                        dve.wait_ge(S(f"tile_used{s % SLOTS}"), s // SLOTS + 1 + i * 2)
                        for c in range(2):
                            x = X[:, bass.ds(4 * i + (2 * half + c), 1), :].rearrange("p o n -> p (o n)")
                            dve.tensor_tensor(x, acc(n, c), x, ALU.add).then_inc(S(f"pair_taken{n % 2}"), 1)
                wait_evacuated(dve, down, 2)
                wait_evacuated(dve, down, 3)

            residual("rec_out")
            dve.memset(small[:, 224:225], 0.0).then_inc(S("hidden"), 1)
            rms_norm("rms_mlp0", "mlp_g", 0)
            mlp(0)
            rms_norm("rms_mix1", "mix_g", 8)
            wait_made(dve, "wi")
            taken(dve.tensor_scalar(WI[:, :, :], bank("wi")[:, 0:16].rearrange("p (t h) -> p t h", t=TT), IDX_W_SCALE, None,
                                    ALU.mult), "wi")
            wait_taken(dve, "rms_c")
            did(dve.reciprocal(RS[:, :], RS[:, :]))
            settle()
            dve.scalar_tensor_tensor(CN, CR, pc("kv_g"), RS[:, :], ALU.mult, ALU.mult).then_inc(S("cn_ready"), 1)

            halves = ((0, P), (P, WIDE))
            for h in range(H_IDX):
                wait_made(dve, ("dot", h))
                b = bank(("dot", h))
                dst = SCW if h == 0 else (TMP, TMP2)[h % 2]
                did(dve.tensor_scalar(dst[:, 0:P], b[:, 0:P], 0.0, WI[:, 0, h:h + 1], ALU.max, ALU.mult))
                taken(dve.tensor_scalar(dst[:, P:WIDE], b[:, P:WIDE], 0.0, WI[:, 1, h:h + 1], ALU.max, ALU.mult), ("dot", h))
                wait_taken(dve, ("dot", h))
                settle()
                if h:
                    did(dve.tensor_tensor(SCW, SCW, dst, ALU.add))
                    settle()
            did(dve.tensor_scalar(MSK, cst("dist"), 0.5 * FAR, None, ALU.is_lt))
            settle()
            did(dve.tensor_scalar(TMP, MSK, -1.0, FAR, ALU.add, ALU.mult))
            did(dve.tensor_tensor(SCW, SCW, MSK, ALU.mult))
            settle()
            did(dve.tensor_tensor(SCW, SCW, TMP, ALU.add))
            settle()
            for r in range(KEEP // 8):
                for x, y in halves:
                    did(dve.max(MX[:, 8 * (x > 0):8 * (x > 0) + 8], SCW[:, x:y]))
                settle()
                for x, y in halves:
                    did(dve.match_replace(SCW[:, x:y], MX[:, 8 * (x > 0):8 * (x > 0) + 8], SCW[:, x:y], NEG))
                settle()
            did(dve.tensor_scalar(SCW, SCW, NEG, None, ALU.is_equal))
            settle()
            did(dve.tensor_tensor(MSK, MSK, SCW, ALU.mult))
            settle()
            did(dve.tensor_scalar(MSK, MSK, -1.0, FAR, ALU.add, ALU.mult))
            settle()
            def logit(h):
                wait_made(dve, ("lg", h))
                p = PR[h % 4]
                if h >= 4:
                    wait_made(dve, ("pt", h - 4))
                b = bank(("lg", h))
                m = MX[:, 2 * (h % 4):2 * (h % 4) + 2]
                did(dve.tensor_tensor_reduce(p[:, 0:P], b[:, 0:P], MSK[:, 0:P], 1.0, NEG, ALU.add, ALU.max, m[:, 0:1]))
                taken(dve.tensor_tensor_reduce(p[:, P:WIDE], b[:, P:WIDE], MSK[:, P:WIDE], 1.0, NEG, ALU.add, ALU.max,
                                               m[:, 1:2]), ("lg", h))
                wait_taken(dve, ("lg", h))
                dve.tensor_scalar(m, m, -1.0, None, ALU.mult).then_inc(S("lg_negmax"), 1)

            logit(0)
            for h in range(H_ATT):
                if h + 1 < H_ATT:
                    logit(h + 1)
                dve.wait_ge(S("lg_exp"), 2 * (h + 1))
                sm = SM[:, 2 * (h % 4):2 * (h % 4) + 2]
                did(dve.reciprocal(sm, sm))
                settle()
                p = PR[h % 4]
                did(dve.tensor_scalar(p[:, 0:P], p[:, 0:P], sm[:, 0:1], None, ALU.mult))
                settle()
                dve.tensor_scalar(p[:, P:WIDE], p[:, P:WIDE], sm[:, 1:2], None, ALU.mult).then_inc(S("p_ready"), 1)
            residual("att_out")
            rms_norm("rms_mlp1", "mlp_g", 8)
            mlp(1)
            rms_norm("rms_fin", "final_g", 0, "out_ready")


def lay_out(np_, inputs):
    a = {k: np_.asarray(v) for k, v in inputs.items()}

    def tiles(w):
        i, o = w.shape
        return w.reshape(i // D, DC, P, o // COLS, COLS).transpose(3, 0, 2, 1, 4).reshape(-1, P, TILE)

    def cols(v):
        return v.reshape(-1, P).T

    w_in = a["w_in"][0]
    q, k, v, z, xbc, dt, g = np_.split(w_in, [1024, 2048, 3072, 5120, 8192, 8224], axis=1)
    att = a["att_w_in_2"][0]
    rec = a["rec_w_in_2"][0]
    ki = att[:, 1664:1728]
    att_cols = np_.concatenate([att[:, 1024:1664], ki, ki, att[:, 0:1024]], axis=1)
    uk = a["att_w_uk_2"][0].reshape(8, P, P).transpose(1, 0, 2).reshape(P, 1024)
    uv = a["att_w_uv_2"][0].transpose(1, 0, 2).reshape(P, 1024)
    parts = [q, k, v, xbc, z, g, a["w_attn_branch"][0], a["w_ssd_branch"][0], a["w_out"][0], a["peer_w_query"][0],
             np_.concatenate([rec[:, 1024:], rec[:, :1024]], axis=1), a["rec_w_out_2"][0], a["mlp_w_up_2"][0], a["mlp_w_down_2"][0], att_cols, None,
             a["att_w_o_2"][0], a["mlp_w_up_2"][1], a["mlp_w_down_2"][1]]
    stream = np_.concatenate([tiles(w) if w is not None else np_.concatenate([uk, uv], axis=1)[None] for w in parts])
    f = np_.float32
    p_, m_ = np_.arange(P), np_.arange(TOK)

    def dist(q0, n):
        d = (q0 + p_[:, None] - np_.arange(n)[None, :]).astype(f)
        return np_.where(d >= 0, d, f(FAR)).astype(f)

    con = np_.concatenate([np_.eye(P, dtype=f), np_.ones((P, P), f), dist(0, P), dist(P, TOK),
                           (p_[:, None] <= m_[None, :]).astype(f), np_.tile(np_.arange(TOPK, dtype=f), (P, 1)),
                           np_.eye(P, dtype=f)[::-1]], axis=1)
    n = np_.maximum(TOK - 1 - np_.arange(WIDE), 0)
    large = 16 + (np_.log(np_.maximum(n, 1).astype(f) / f(16)) / f(math.log(8.0)) * f(16)).astype(np_.int32)
    bucket = np_.where(n < 16, n, np_.minimum(large, BUCKETS - 1))
    rg = np_.stack([a["rec_w_a_2"][0], a["rec_w_x_2"][0]]).reshape(2, 8, P, 256).transpose(2, 0, 1, 3).reshape(P, 4096)
    par = [a["b_ada"], a["conv_w"][0], a["conv_b"], a["ssd_norm_w"], np_.repeat(a["d_skip"][0], 64), a["da_subln_w"],
           a["ln1_g"], a["ln1_b"], a["ln2_g"], a["ln2_b"], a["norm_mix_g_2"], a["norm_mlp_g_2"], a["final_norm_g_2"],
           a["rec_conv_w_2"][0], a["rec_conv_b_2"], a["rec_b_a_2"], a["rec_b_x_2"], a["rec_lambda_2"],
           a["att_kv_norm_g_2"], a["c"]]
    rows = np_.concatenate([a[x][0] for x, _ in ROWS])
    return {
        "stream": stream,
        "ada": tiles(a["w_ada"][0]),
        "par": np_.concatenate([cols(x) for x in par], axis=1),
        "rows": np_.tile(rows, (P, 1)),
        "con": con,
        "xT": a["x"][0].T.reshape(DC, P, TOK).transpose(1, 0, 2),
        "wdt": dt.reshape(DC, P, 32).transpose(1, 0, 2),
        "sk": a["peer_sub_keys"][0].transpose(2, 0, 1).reshape(P, 2 * P),
        "peer_uv": np_.concatenate([a["peer_u"][0], a["peer_v"][0]], axis=1),
        "rgw": rg,
        "wwi": att[:, 1728:1736].reshape(DC, P, 8).transpose(1, 0, 2),
        "selh": (np_.arange(BUCKETS)[:, None] == bucket[None, :]).astype(f),
        "relb": a["rel_bias_2"],
    }


def kernel(**inputs):
    import numpy as _np
    import concourse.bacc as _bacc
    from concourse import mybir as _mybir
    from concourse.bass_utils import run_bass_kernel_spmd as _run

    nc = _bacc.Bacc("TRN2", target_bir_lowering=False, num_devices=1)
    arrays, io = {}, {}
    for name, a in lay_out(_np, inputs).items():
        a = _np.ascontiguousarray(a)
        arrays[f"in_{name}_dram"] = a
        io[name] = nc.dram_tensor(f"in_{name}_dram", a.shape, _mybir.dt.from_np(a.dtype), kind="ExternalInput").ap()
    io["bv"] = nc.dram_tensor("bias_by_distance", (H_ATT, WIDE), F32, kind="Internal").ap()
    io["outT"] = nc.dram_tensor("out_0_dram", (P, DC, TOK), F32, kind="ExternalOutput").ap()
    program(nc, io)
    r = _run(nc, [arrays], core_ids=[0])
    out = r.results[0]["out_0_dram"]
    return out.transpose(2, 1, 0).reshape(1, TOK, D)
```
